# Optimizing a Trainium2 kernel written in Bass

```python
import numpy as np
import jax, jax.numpy as jnp
from jax import lax
import math

D_MODEL = 1024
BATCH = 1
SEQ = 512
DEPTH = 1

D_CONV = D_MODEL
CONV_K = 3
HEAD_DIM = 64
N_HEADS = D_MODEL // HEAD_DIM
N_KV_HEADS = 4
GROUP = N_HEADS // N_KV_HEADS
D_ATTN = N_HEADS * HEAD_DIM
D_KV = N_KV_HEADS * HEAD_DIM
WINDOW = 128
BLOCK = 128
ROPE_THETA = 10000.0
D_FF = 2816
N_MOD = 9
EPS = 1e-6
ADA_INIT = 0.5
NEG_INF = -1e30

IN_SPLITS = [D_CONV, D_CONV, D_CONV, D_ATTN, D_KV, D_KV, D_MODEL, D_MODEL]
IN_OFFSETS = [int(o) for o in np.cumsum(IN_SPLITS)[:-1]]
D_IN = int(sum(IN_SPLITS))


def rms_norm(x, g):
    xf = x.astype(jnp.float32)
    y = xf * lax.rsqrt(jnp.mean(xf * xf, axis=-1, keepdims=True) + EPS)
    return (y * g.astype(jnp.float32)).astype(x.dtype)

def modulate(h, shift, scale):
    return h * (1 + scale[:, None, :]) + shift[:, None, :]

def swiglu(h, w_gu, w_down):
    a, b = jnp.split(h @ w_gu, 2, axis=-1)
    return (jax.nn.silu(a) * b) @ w_down

def rope_tables(seq):
    inv = 1.0 / (ROPE_THETA ** (jnp.arange(0, HEAD_DIM, 2, dtype=jnp.float32) / HEAD_DIM))
    ang = jnp.arange(seq, dtype=jnp.float32)[:, None] * inv[None, :]
    return jnp.cos(ang), jnp.sin(ang)

def apply_rope(t, cos, sin):
    t1, t2 = jnp.split(t.astype(jnp.float32), 2, axis=-1)
    c = cos[None, :, None, :]
    s = sin[None, :, None, :]
    return jnp.concatenate([t1 * c - t2 * s, t2 * c + t1 * s], axis=-1).astype(t.dtype)

def short_conv(u, w):
    s = u.shape[1]
    up = jnp.pad(u, ((0, 0), (CONV_K - 1, 0), (0, 0)))
    out = up[:, 0:s] * w[0]
    for j in range(1, CONV_K):
        out = out + up[:, j:j + s] * w[j]
    return out

def sliding_window_attention(q, k, v, sinks):
    bsz, s, _, _ = q.shape
    nb = s // BLOCK
    qb = q.reshape(bsz, nb, BLOCK, N_KV_HEADS, GROUP, HEAD_DIM)

    def band(t):
        tp = jnp.pad(t, ((0, 0), (BLOCK, 0), (0, 0), (0, 0)))
        tp = tp.reshape(bsz, nb + 1, BLOCK, N_KV_HEADS, HEAD_DIM)
        return jnp.concatenate([tp[:, :-1], tp[:, 1:]], axis=2)

    kb, vb = band(k), band(v)
    scores = jnp.einsum('bnqhgd,bnkhd->bnhgqk', qb, kb,
                        preferred_element_type=jnp.float32) * (HEAD_DIM ** -0.5)
    qi = jnp.arange(BLOCK)[:, None]
    kj = jnp.arange(2 * BLOCK)[None, :]
    diff = BLOCK + qi - kj
    in_window = (diff >= 0) & (diff < WINDOW)
    k_pos = (jnp.arange(nb)[:, None] - 1) * BLOCK + jnp.arange(2 * BLOCK)[None, :]
    valid = in_window[None] & (k_pos >= 0)[:, None, :]
    scores = jnp.where(valid[None, :, None, None], scores, NEG_INF)
    sink = sinks.astype(jnp.float32).reshape(N_KV_HEADS, GROUP)[None, None, :, :, None, None]
    m = jnp.maximum(jnp.max(scores, axis=-1, keepdims=True), sink)
    p = jnp.exp(scores - m)
    denom = jnp.sum(p, axis=-1, keepdims=True) + jnp.exp(sink - m)
    probs = (p / denom).astype(v.dtype)
    out = jnp.einsum('bnhgqk,bnkhd->bnqhgd', probs, vb)
    return out.reshape(bsz, s, D_ATTN)

def first_inputs(seed: int = 0) -> dict:
    key = jax.random.key(seed)
    ks = jax.random.split(key, 24)
    f32 = jnp.float32

    def nrm(k, shape, fan_in, mult=1.0):
        return jax.random.normal(k, shape, f32) * (mult * fan_in ** -0.5)

    def gain(k, shape):
        return 1.0 + 0.05 * jax.random.normal(k, shape, f32)

    L = DEPTH
    return {
        "x": jax.random.normal(ks[0], (BATCH, SEQ, D_MODEL), f32),
        "c": jax.random.normal(ks[1], (BATCH, D_MODEL), f32),
        "w_ada": nrm(ks[2], (L, D_MODEL, N_MOD * D_MODEL), D_MODEL, ADA_INIT),
        "b_ada": 0.02 * jax.random.normal(ks[3], (L, N_MOD * D_MODEL), f32),
        "g_ffn1": gain(ks[4], (L, D_MODEL)),
        "w1_gu": nrm(ks[5], (L, D_MODEL, 2 * D_FF), D_MODEL),
        "w1_down": nrm(ks[6], (L, D_FF, D_MODEL), D_FF),
        "g_mix": gain(ks[7], (L, D_MODEL)),
        "w_in": nrm(ks[8], (L, D_MODEL, D_IN), D_MODEL),
        "conv_w": nrm(ks[9], (L, CONV_K, D_CONV), CONV_K),
        "w_conv_proj": nrm(ks[10], (L, D_CONV, D_MODEL), D_CONV),
        "w_attn_proj": nrm(ks[11], (L, D_ATTN, D_MODEL), D_ATTN),
        "sinks": jax.random.normal(ks[12], (L, N_HEADS), f32),
        "w_out": nrm(ks[13], (L, D_MODEL, D_MODEL), D_MODEL),
        "g_ffn2": gain(ks[14], (L, D_MODEL)),
        "w2_gu": nrm(ks[15], (L, D_MODEL, 2 * D_FF), D_MODEL),
        "w2_down": nrm(ks[16], (L, D_FF, D_MODEL), D_FF),
        "g_final": gain(ks[17], (D_MODEL,)),
    }

def first_block(x, c, w_ada, b_ada, g_ffn1, w1_gu, w1_down, g_mix, w_in, conv_w,
              w_conv_proj, w_attn_proj, sinks, w_out, g_ffn2, w2_gu, w2_down, g_final):
    bsz, s, _ = x.shape
    cos, sin = rope_tables(s)
    c_act = jax.nn.silu(c)
    for l in range(DEPTH):
        mods = jnp.split(c_act @ w_ada[l] + b_ada[l], N_MOD, axis=-1)
        sh1, sc1, gt1, sh2, sc2, gt2, sh3, sc3, gt3 = mods

        h = modulate(rms_norm(x, g_ffn1[l]), sh1, sc1)
        x = x + 0.5 * gt1[:, None, :] * swiglu(h, w1_gu[l], w1_down[l])

        h = modulate(rms_norm(x, g_mix[l]), sh2, sc2)
        proj = h @ w_in[l]
        b_g, c_g, u, q, k, v, z_conv, z_attn = jnp.split(proj, IN_OFFSETS, axis=-1)

        y_conv = (b_g * short_conv(c_g * u, conv_w[l])) @ w_conv_proj[l]

        q = apply_rope(q.reshape(bsz, s, N_HEADS, HEAD_DIM), cos, sin)
        k = apply_rope(k.reshape(bsz, s, N_KV_HEADS, HEAD_DIM), cos, sin)
        v = v.reshape(bsz, s, N_KV_HEADS, HEAD_DIM)
        y_attn = sliding_window_attention(q, k, v, sinks[l]) @ w_attn_proj[l]

        merged = jax.nn.sigmoid(z_conv) * y_conv + jax.nn.sigmoid(z_attn) * y_attn
        x = x + gt2[:, None, :] * (merged @ w_out[l])

        h = modulate(rms_norm(x, g_ffn2[l]), sh3, sc3)
        x = x + 0.5 * gt3[:, None, :] * swiglu(h, w2_gu[l], w2_down[l])

    return rms_norm(x, g_final)


MIX_WIDTH = D_MODEL
NSA_WIDTH = MIX_WIDTH // 2
NSA_HEAD_DIM = 64
NSA_HEADS = NSA_WIDTH // NSA_HEAD_DIM
NSA_KV_HEADS = 2
NSA_GROUP = NSA_HEADS // NSA_KV_HEADS
NSA_KV_WIDTH = NSA_KV_HEADS * NSA_HEAD_DIM
CMP_STRIDE = 16
CMP_BLOCK = 2 * CMP_STRIDE
CMP_HIDDEN = 4 * NSA_HEAD_DIM
SEL_BLOCK = 64
N_SELECT = 16
WINDOW_2 = 512
Q_BLOCK = 128
FORCED_SCORE = 1.0e4
MLSTM_WIDTH = MIX_WIDTH - NSA_WIDTH
MLSTM_HEADS = 4
MLSTM_V_DIM = MLSTM_WIDTH // MLSTM_HEADS
MLSTM_QK_DIM = MLSTM_V_DIM // 2
MLSTM_QK_WIDTH = MLSTM_HEADS * MLSTM_QK_DIM
MLSTM_CHUNK = 64
CONV_WIDTH = 4
REL_BUCKETS = 32
REL_MAX_DISTANCE = 128
MEM_TOKENS = 256
XATTN_HEADS = 4
XATTN_HEAD_DIM = D_MODEL // XATTN_HEADS
D_FF_2 = -(-8 * D_MODEL // (3 * 256)) * 256
NORM_EPS = 1e-6
NEG_INF_2 = -1.0e30

IN_SIZES = (NSA_WIDTH,) + (NSA_KV_WIDTH,) * 6 + (NSA_HEADS * 3, MLSTM_QK_WIDTH, MLSTM_QK_WIDTH,
            MLSTM_WIDTH, MLSTM_HEADS, MLSTM_HEADS, MLSTM_WIDTH)
IN_WIDTH = sum(IN_SIZES)
IN_OFFSETS_2 = tuple(int(o) for o in np.cumsum(IN_SIZES)[:-1])


def rms_norm_2(x, gain):
    xf = x.astype(jnp.float32)
    y = xf * lax.rsqrt(jnp.mean(xf * xf, axis=-1, keepdims=True) + NORM_EPS)
    return (y * gain.astype(jnp.float32)).astype(x.dtype)

def rel_bucket(dist):
    n = jnp.maximum(dist, 0)
    max_exact = REL_BUCKETS // 2
    nf = jnp.maximum(n, 1).astype(jnp.float32)
    large = max_exact + (jnp.log(nf / max_exact) / math.log(REL_MAX_DISTANCE / max_exact)
                         * (REL_BUCKETS - max_exact)).astype(jnp.int32)
    large = jnp.minimum(large, REL_BUCKETS - 1)
    return jnp.where(n < max_exact, n, large)

def masked_softmax(s, mask):
    s = jnp.where(mask, s.astype(jnp.float32), NEG_INF_2)
    return jnp.where(mask, jax.nn.softmax(s, axis=-1), 0.0)

def compress_blocks(kv, pos, w1, w2):
    B, H, S, DH = kv.shape
    c = kv.reshape(B, H, S // CMP_STRIDE, CMP_STRIDE, DH)
    blocks = jnp.concatenate([c[:, :, :-1], c[:, :, 1:]], axis=3) + pos
    hid = jax.nn.silu(blocks.reshape(B, H, -1, CMP_BLOCK * DH) @ w1)
    return hid @ w2

def native_sparse_attention(q, k_cmp, v_cmp, k_slc, v_slc, k_win, v_win, gates, rel_bias):
    B, HKV, G, S, DH = q.shape
    n_cmp = k_cmp.shape[2]
    n_sel = S // SEL_BLOCK
    n_top = min(N_SELECT, n_sel)
    n_kwin = Q_BLOCK + WINDOW_2
    cmp_start = jnp.arange(n_cmp) * CMP_STRIDE
    cmp_end = cmp_start + (CMP_BLOCK - 1)
    sel_start = jnp.arange(n_sel) * SEL_BLOCK
    overlap = ((cmp_start[:, None] <= sel_start[None, :] + SEL_BLOCK - 1)
               & (cmp_end[:, None] >= sel_start[None, :])).astype(jnp.float32)
    k_blk = k_slc.reshape(B, HKV, n_sel, SEL_BLOCK, DH)
    v_blk = v_slc.reshape(B, HKV, n_sel, SEL_BLOCK, DH)
    k_pad = jnp.pad(k_win, ((0, 0), (0, 0), (WINDOW_2, 0), (0, 0)))
    v_pad = jnp.pad(v_win, ((0, 0), (0, 0), (WINDOW_2, 0), (0, 0)))
    gather = jax.vmap(jax.vmap(lambda blocks, idx: blocks[idx]))
    head_off = (jnp.arange(NSA_HEADS) * REL_BUCKETS).reshape(HKV, G)
    bias_flat = rel_bias.reshape(-1)
    blk_ids = jnp.arange(n_sel)

    def head_bias(dist):
        return rel_bias[:, rel_bucket(dist)].reshape(HKV, G, *dist.shape)

    def query_block(c):
        t0 = c * Q_BLOCK
        tq = t0 + jnp.arange(Q_BLOCK)
        qc = lax.dynamic_slice_in_dim(q, t0, Q_BLOCK, axis=3)
        gc = lax.dynamic_slice_in_dim(gates, t0, Q_BLOCK, axis=3)
        d_c = tq[:, None] - cmp_end[None, :]
        s_c = jnp.einsum('bhgtd,bhcd->bhgtc', qc, k_cmp).astype(jnp.float32) + head_bias(d_c)
        p_c = masked_softmax(s_c, d_c >= 0)
        o_c = jnp.einsum('bhgtc,bhcd->bhgtd', p_c.astype(v_cmp.dtype), v_cmp)
        imp = jnp.einsum('bhgtc,cj->bhtj', p_c, overlap)
        cur = tq // SEL_BLOCK
        forced = ((blk_ids[None, :] == 0) | (blk_ids[None, :] == cur[:, None])
                  | (blk_ids[None, :] == cur[:, None] - 1))
        score = jnp.where(forced, FORCED_SCORE, jnp.where(blk_ids[None, :] <= cur[:, None], imp, -1.0))
        _, idx = lax.top_k(score, n_top)
        k_s = gather(k_blk, idx).reshape(B, HKV, Q_BLOCK, n_top * SEL_BLOCK, DH)
        v_s = gather(v_blk, idx).reshape(B, HKV, Q_BLOCK, n_top * SEL_BLOCK, DH)
        kpos = (idx[..., None] * SEL_BLOCK + jnp.arange(SEL_BLOCK)).reshape(B, HKV, Q_BLOCK, n_top * SEL_BLOCK)
        d_s = tq[:, None] - kpos
        b_s = bias_flat[head_off[None, :, :, None, None] + rel_bucket(d_s)[:, :, None]]
        s_s = jnp.einsum('bhgtd,bhtkd->bhgtk', qc, k_s).astype(jnp.float32) + b_s
        p_s = masked_softmax(s_s, (d_s >= 0)[:, :, None])
        o_s = jnp.einsum('bhgtk,bhtkd->bhgtd', p_s.astype(v_s.dtype), v_s)
        k_w = lax.dynamic_slice_in_dim(k_pad, t0, n_kwin, axis=2)
        v_w = lax.dynamic_slice_in_dim(v_pad, t0, n_kwin, axis=2)
        kpos_w = t0 - WINDOW_2 + jnp.arange(n_kwin)
        d_w = tq[:, None] - kpos_w[None, :]
        m_w = (d_w >= 0) & (d_w < WINDOW_2) & (kpos_w[None, :] >= 0)
        s_w = jnp.einsum('bhgtd,bhkd->bhgtk', qc, k_w).astype(jnp.float32) + head_bias(d_w)
        p_w = masked_softmax(s_w, m_w)
        o_w = jnp.einsum('bhgtk,bhkd->bhgtd', p_w.astype(v_w.dtype), v_w)
        return gc[..., 0:1] * o_c + gc[..., 1:2] * o_s + gc[..., 2:3] * o_w

    return lax.map(query_block, jnp.arange(S // Q_BLOCK))

def causal_depthwise_conv(u, w, b):
    y = lax.conv_general_dilated(u, w[:, None, :].astype(u.dtype), window_strides=(1,),
                                 padding=((CONV_WIDTH - 1, 0),), dimension_numbers=('NWC', 'WIO', 'NWC'),
                                 feature_group_count=u.shape[-1])
    return y + b

def mlstm_chunkwise(q, k, v, i_pre, log_f):
    B, S, H, DK = q.shape
    DV = v.shape[-1]
    L = MLSTM_CHUNK
    nc = S // L
    f32 = jnp.float32

    def chunks(t):
        return t.astype(f32).reshape(B, nc, L, H, -1).transpose(1, 0, 3, 2, 4)

    qs, ks, vs = chunks(q), chunks(k) * (DK ** -0.5), chunks(v)
    ig = chunks(i_pre[..., None])[..., 0]
    lf = chunks(log_f[..., None])[..., 0]
    causal = jnp.tril(jnp.ones((L, L), dtype=bool))

    def step(carry, inp):
        C, n, m = carry
        qc, kc, vc, ic, fc = inp
        b = jnp.cumsum(fc, axis=-1)
        D = jnp.where(causal, b[..., :, None] - b[..., None, :] + ic[..., None, :], NEG_INF_2)
        m_inter = b + m[..., None]
        m_t = jnp.maximum(m_inter, jnp.max(D, axis=-1))
        w = jnp.exp(D - m_t[..., None])
        a = jnp.exp(m_inter - m_t)
        s = jnp.einsum('bhtd,bhsd->bhts', qc, kc) * w
        num = jnp.einsum('bhts,bhsv->bhtv', s, vc) + a[..., None] * jnp.einsum('bhtd,bhdv->bhtv', qc, C)
        den = jnp.sum(s, axis=-1) + a * jnp.einsum('bhtd,bhd->bht', qc, n)
        h = num / jnp.maximum(jnp.abs(den), jnp.exp(-m_t))[..., None]
        bL = b[..., -1]
        ws = bL[..., None] - b + ic
        m_next = jnp.maximum(bL + m, jnp.max(ws, axis=-1))
        decay = jnp.exp(bL + m - m_next)
        kw = kc * jnp.exp(ws - m_next[..., None])[..., None]
        C = decay[..., None, None] * C + jnp.einsum('bhsd,bhsv->bhdv', kw, vc)
        n = decay[..., None] * n + jnp.sum(kw, axis=2)
        return (C, n, m_next), h

    init = (jnp.zeros((B, H, DK, DV), f32), jnp.zeros((B, H, DK), f32), jnp.zeros((B, H), f32))
    _, hs = lax.scan(step, init, (qs, ks, vs, ig, lf))
    return hs.transpose(1, 0, 3, 2, 4).reshape(B, S, H, DV)

def hybrid_mixer(h, rel_bias, w_in, cmp_pos_k, cmp_pos_v, cmp_w1_k, cmp_w2_k, cmp_w1_v, cmp_w2_v,
                 conv_w, conv_b, mlstm_gate_bias, mlstm_norm, w_out):
    B, S, _ = h.shape
    (nq, kc, vc, ksl, vsl, kwn, vwn, gt, mq, mk, mv, mi, mf, mo) = jnp.split(h @ w_in, IN_OFFSETS_2, axis=-1)

    def kv_heads(t):
        return t.reshape(B, S, NSA_KV_HEADS, NSA_HEAD_DIM).transpose(0, 2, 1, 3)

    q = nq.reshape(B, S, NSA_KV_HEADS, NSA_GROUP, NSA_HEAD_DIM).transpose(0, 2, 3, 1, 4) * (NSA_HEAD_DIM ** -0.5)
    k_cmp = compress_blocks(kv_heads(kc), cmp_pos_k, cmp_w1_k, cmp_w2_k)
    v_cmp = compress_blocks(kv_heads(vc), cmp_pos_v, cmp_w1_v, cmp_w2_v)
    gates = jax.nn.sigmoid(gt.reshape(B, S, NSA_KV_HEADS, NSA_GROUP, 3).transpose(0, 2, 3, 1, 4))
    o = native_sparse_attention(q, k_cmp, v_cmp, kv_heads(ksl), kv_heads(vsl), kv_heads(kwn), kv_heads(vwn),
                                gates, rel_bias)
    y_nsa = o.transpose(1, 0, 4, 2, 3, 5).reshape(B, S, NSA_WIDTH)

    qk = jax.nn.silu(causal_depthwise_conv(jnp.concatenate([mq, mk], axis=-1), conv_w, conv_b))
    mq, mk = jnp.split(qk, 2, axis=-1)
    hm = mlstm_chunkwise(mq.reshape(B, S, MLSTM_HEADS, MLSTM_QK_DIM), mk.reshape(B, S, MLSTM_HEADS, MLSTM_QK_DIM),
                         mv.reshape(B, S, MLSTM_HEADS, MLSTM_V_DIM),
                         mi.astype(jnp.float32) + mlstm_gate_bias[0].astype(jnp.float32),
                         jax.nn.log_sigmoid(mf.astype(jnp.float32) + mlstm_gate_bias[1].astype(jnp.float32)))
    hm = hm * lax.rsqrt(jnp.mean(hm * hm, axis=-1, keepdims=True) + NORM_EPS)
    hm = (hm.reshape(B, S, MLSTM_WIDTH) * mlstm_norm.astype(jnp.float32)).astype(h.dtype)
    y_ml = jax.nn.sigmoid(mo) * hm

    return jnp.concatenate([y_nsa, y_ml], axis=-1) @ w_out

def memory_cross_attention(h, mem_n, w_xq, w_xkv, w_xo):
    B, S, _ = h.shape
    M = mem_n.shape[1]
    q = (h @ w_xq).reshape(B, S, XATTN_HEADS, XATTN_HEAD_DIM) * (XATTN_HEAD_DIM ** -0.5)
    k, v = jnp.split(mem_n @ w_xkv, 2, axis=-1)
    k = k.reshape(B, M, XATTN_HEADS, XATTN_HEAD_DIM)
    v = v.reshape(B, M, XATTN_HEADS, XATTN_HEAD_DIM)
    p = jax.nn.softmax(jnp.einsum('bshd,bmhd->bhsm', q, k).astype(jnp.float32), axis=-1)
    o = jnp.einsum('bhsm,bmhd->bshd', p.astype(v.dtype), v).reshape(B, S, D_MODEL)
    return o @ w_xo

def swiglu_ffn(h, w_gate_up, w_down):
    g, u = jnp.split(h @ w_gate_up, 2, axis=-1)
    return (jax.nn.silu(g) * u) @ w_down

def second_inputs(seed: int = 0) -> dict:
    key = jax.random.key(seed)
    keys = iter(jax.random.split(key, 40))

    def nrm(shape, scale):
        return scale * jax.random.normal(next(keys), shape, jnp.float32)

    def gain(width=D_MODEL):
        return 1.0 + nrm((DEPTH, width), 0.02)

    inputs = {}
    inputs['x'] = nrm((BATCH, SEQ, D_MODEL), 1.0)
    inputs['mem'] = nrm((BATCH, MEM_TOKENS, D_MODEL), 1.0)
    inputs['rel_bias'] = nrm((NSA_HEADS, REL_BUCKETS), 0.5)
    inputs['mix_norm_pre'] = gain()
    inputs['w_in'] = nrm((DEPTH, D_MODEL, IN_WIDTH), D_MODEL ** -0.5)
    inputs['cmp_pos_k'] = nrm((DEPTH, CMP_BLOCK, NSA_HEAD_DIM), 0.02)
    inputs['cmp_pos_v'] = nrm((DEPTH, CMP_BLOCK, NSA_HEAD_DIM), 0.02)
    inputs['cmp_w1_k'] = nrm((DEPTH, CMP_BLOCK * NSA_HEAD_DIM, CMP_HIDDEN), (CMP_BLOCK * NSA_HEAD_DIM) ** -0.5)
    inputs['cmp_w2_k'] = nrm((DEPTH, CMP_HIDDEN, NSA_HEAD_DIM), CMP_HIDDEN ** -0.5)
    inputs['cmp_w1_v'] = nrm((DEPTH, CMP_BLOCK * NSA_HEAD_DIM, CMP_HIDDEN), (CMP_BLOCK * NSA_HEAD_DIM) ** -0.5)
    inputs['cmp_w2_v'] = nrm((DEPTH, CMP_HIDDEN, NSA_HEAD_DIM), CMP_HIDDEN ** -0.5)
    inputs['conv_w'] = nrm((DEPTH, CONV_WIDTH, 2 * MLSTM_QK_WIDTH), CONV_WIDTH ** -0.5)
    inputs['conv_b'] = nrm((DEPTH, 2 * MLSTM_QK_WIDTH), 0.01)
    forget_bias = jnp.broadcast_to(jnp.linspace(3.0, 6.0, MLSTM_HEADS), (DEPTH, MLSTM_HEADS))
    inputs['mlstm_gate_bias'] = jnp.stack([nrm((DEPTH, MLSTM_HEADS), 0.1),
                                           forget_bias + nrm((DEPTH, MLSTM_HEADS), 0.1)], axis=1)
    inputs['mlstm_norm'] = gain(MLSTM_WIDTH)
    inputs['w_out'] = nrm((DEPTH, MIX_WIDTH, D_MODEL), MIX_WIDTH ** -0.5)
    inputs['mix_norm_post'] = gain()
    inputs['xattn_norm_pre'] = gain()
    inputs['mem_norm'] = gain()
    inputs['w_xq'] = nrm((DEPTH, D_MODEL, D_MODEL), D_MODEL ** -0.5)
    inputs['w_xkv'] = nrm((DEPTH, D_MODEL, 2 * D_MODEL), D_MODEL ** -0.5)
    inputs['w_xo'] = nrm((DEPTH, D_MODEL, D_MODEL), D_MODEL ** -0.5)
    inputs['xattn_norm_post'] = gain()
    inputs['ffn_norm_pre'] = gain()
    inputs['w_gate_up'] = nrm((DEPTH, D_MODEL, 2 * D_FF_2), D_MODEL ** -0.5)
    inputs['w_down'] = nrm((DEPTH, D_FF_2, D_MODEL), D_FF_2 ** -0.5)
    inputs['ffn_norm_post'] = gain()
    return inputs

def second_block(x, mem, rel_bias, mix_norm_pre, w_in, cmp_pos_k, cmp_pos_v, cmp_w1_k, cmp_w2_k, cmp_w1_v,
              cmp_w2_v, conv_w, conv_b, mlstm_gate_bias, mlstm_norm, w_out, mix_norm_post, xattn_norm_pre,
              mem_norm, w_xq, w_xkv, w_xo, xattn_norm_post, ffn_norm_pre, w_gate_up, w_down, ffn_norm_post):
    for l in range(DEPTH):
        h = rms_norm_2(x, mix_norm_pre[l])
        y = hybrid_mixer(h, rel_bias, w_in[l], cmp_pos_k[l], cmp_pos_v[l], cmp_w1_k[l], cmp_w2_k[l],
                         cmp_w1_v[l], cmp_w2_v[l], conv_w[l], conv_b[l], mlstm_gate_bias[l], mlstm_norm[l], w_out[l])
        x = x + rms_norm_2(y, mix_norm_post[l])
        h = rms_norm_2(x, xattn_norm_pre[l])
        y = memory_cross_attention(h, rms_norm_2(mem, mem_norm[l]), w_xq[l], w_xkv[l], w_xo[l])
        x = x + rms_norm_2(y, xattn_norm_post[l])
        h = rms_norm_2(x, ffn_norm_pre[l])
        y = swiglu_ffn(h, w_gate_up[l], w_down[l])
        x = x + rms_norm_2(y, ffn_norm_post[l])
    return x


def setup_inputs(seed=0):
    out = dict(first_inputs(seed))
    for name, value in second_inputs(seed + 1).items():
        if name != "x":
            out[name + "_2"] = value
    return out


def reference(
    x, c, w_ada, b_ada, g_ffn1, w1_gu, w1_down, g_mix, w_in, conv_w, w_conv_proj, w_attn_proj,
    sinks, w_out, g_ffn2, w2_gu, w2_down, g_final, mem_2, rel_bias_2, mix_norm_pre_2, w_in_2,
    cmp_pos_k_2, cmp_pos_v_2, cmp_w1_k_2, cmp_w2_k_2, cmp_w1_v_2, cmp_w2_v_2, conv_w_2,
    conv_b_2, mlstm_gate_bias_2, mlstm_norm_2, w_out_2, mix_norm_post_2, xattn_norm_pre_2,
    mem_norm_2, w_xq_2, w_xkv_2, w_xo_2, xattn_norm_post_2, ffn_norm_pre_2, w_gate_up_2,
    w_down_2, ffn_norm_post_2,
):
    x = first_block(
        x, c, w_ada, b_ada, g_ffn1, w1_gu, w1_down, g_mix, w_in, conv_w, w_conv_proj,
        w_attn_proj, sinks, w_out, g_ffn2, w2_gu, w2_down, g_final,
    )
    return second_block(
        x, mem_2, rel_bias_2, mix_norm_pre_2, w_in_2, cmp_pos_k_2, cmp_pos_v_2, cmp_w1_k_2,
        cmp_w2_k_2, cmp_w1_v_2, cmp_w2_v_2, conv_w_2, conv_b_2, mlstm_gate_bias_2, mlstm_norm_2,
        w_out_2, mix_norm_post_2, xattn_norm_pre_2, mem_norm_2, w_xq_2, w_xkv_2, w_xo_2,
        xattn_norm_post_2, ffn_norm_pre_2, w_gate_up_2, w_down_2, ffn_norm_post_2,
    )


_drawn_inputs = setup_inputs


def setup_inputs(seed=0):
    import zlib

    import numpy as np

    out = dict(_drawn_inputs(seed))
    spreads = {}
    factors = {'g_ffn1': 4.738,
     'sinks': 8.0,
     'g_ffn2': 4.909,
     'cmp_pos_k_2': 52.788,
     'cmp_pos_v_2': 7.582,
     'conv_b_2': 6.631,
     'mlstm_norm_2': 3.897,
     'mix_norm_post_2': 3.607,
     'xattn_norm_pre_2': 4.443,
     'mem_norm_2': 2.742,
     'xattn_norm_post_2': 13.285,
     'ffn_norm_pre_2': 11.202,
     'ffn_norm_post_2': 22.535}
    for name, (base, spread) in spreads.items():
        noise = np.random.default_rng([zlib.crc32(name.encode()), seed]).standard_normal(out[name].shape)
        drawn = base * np.exp(spread * noise) if base else spread * noise
        out[name] = __import__('jax').numpy.asarray(drawn.astype(out[name].dtype))
    for name, factor in factors.items():
        out[name] = (out[name] * factor).astype(out[name].dtype)
    return out
```

```python
from contextlib import ExitStack

import numpy as np

import concourse.bass as bass
from concourse import mybir

F32 = mybir.dt.float32
F32R = mybir.dt.float32r
ALU = mybir.AluOpType
ACT = mybir.ActivationFunctionType
AX = mybir.AxisListType.X

P = 128
S = 512
D = 1024
DT = D // P
NT = S // P
FF = 2816
FT = FF // P
MEM = 256
HD = 64
NEG = -1e30
EPS = 1e-6
THIRDS = (8, 8, 6)
BLOCK = P * DT * 2 * P

SECTIONS = (("ffn1", 34), ("conv", 12), ("zconv", 8), ("q", 4), ("k", 1), ("v", 1), ("zattn", 8),
            ("out1", 4), ("ffn2", 34), ("misc", 1), ("kvc", 1), ("vv", 1), ("kk", 1), ("nq", 2),
            ("mq", 1), ("mk", 1), ("mv", 2), ("mo", 2), ("cmp", 4), ("out2", 4), ("memk", 4),
            ("memv", 4), ("xq", 4), ("xo", 4), ("ffn3", 34))
AT, NB = {}, 0
for _name, _n in SECTIONS:
    AT[_name] = NB
    NB += _n
ADA_BLOCKS = 9 * DT // 2
START = 2


def done(b):
    return b + START + 1


def used(b):
    return b + START + 1 - (4 if not isinstance(b, int) or b >= AT["cmp"] + 4 else
                            max(0, b - AT["cmp"] + 1))


COLS = (("c", 8), ("b_ada", 72), ("g_ffn1", 8), ("g_mix", 8), ("g_ffn2", 8), ("g_final", 8),
        ("conv", 24), ("mixpre", 8), ("mixpost", 8), ("xpre", 8), ("memn", 8), ("xpost", 8),
        ("fpre", 8), ("fpost", 8), ("conv2", 16), ("conv2b", 4), ("mlnorm", 4), ("pos_k", 16),
        ("pos_v", 16), ("sinks", 16), ("gate_bias", 2))
CAT, NCOL = {}, 0
for _name, _n in COLS:
    CAT[_name] = NCOL
    NCOL += _n
CONSTS = (("ident", 128), ("rot", 128), ("swap", 128), ("tri", 512), ("cos", 512), ("sin", 512),
          ("mask", 256), ("maskT", 128), ("valid", 1))
KAT, NCONST = {}, 0
for _name, _n in CONSTS:
    KAT[_name] = NCONST
    NCONST += _n
NDIST = S + P


class Steps:

    def __init__(self, sem, names):
        self.sem, self.names, self.given = sem, names, 0
        assert len(set(names)) == len(names)

    def one(self, name):
        assert self.names[self.given] == name, (name, self.names[self.given])
        self.given += 1
        return 1

    def at(self, name):
        return self.names.index(name) + 1


def build(nc, ten):
    ctx = ExitStack()
    with ctx:
        def sem(name):
            return ctx.enter_context(nc.semaphore(name))

        def alloc(stack, name, shape, dt=F32):
            return stack.enter_context(nc.sbuf_tensor(name, shape, dt))

        def sb(name, shape, dt=F32):
            return alloc(ctx, name, shape, dt)

        x = sb("x", [P, DT, S])
        act_hi, act_lo = sb("act_hi", [P, DT, S], F32R), sb("act_lo", [P, DT, S], F32R)
        raw = [sb(f"raw{k}", [P, DT, 256]) for k in range(2)]
        w_hi = [sb(f"w_hi{k}", [P, DT, 256], F32R) for k in range(2)]
        w_lo = [sb(f"w_lo{k}", [P, DT, 256], F32R) for k in range(2)]
        cols = sb("cols", [P, NCOL])
        consts = sb("consts", [P, NCONST])
        mods = sb("mods", [P, 72])
        gains = sb("gains", [P, 5, DT])
        negsink = sb("negsink", [P, 16])
        zeros = sb("zeros", [P, 256])
        c_act = sb("c_act", [P, DT])
        ones = sb("ones", [P, P])
        eps = sb("eps", [P, 1])
        normed = [sb(f"normed{k}", [P, S]) for k in range(2)]
        act32 = [sb(f"act32_{k}", [P, S]) for k in range(2)]
        square = [sb(f"square{k}", [P, S]) for k in range(2)]
        sumsq = sb("sumsq", [P, S])
        root, rinv = sb("root", [P, NT]), sb("rinv", [P, NT])
        w2 = sb("w2", [P, 2, 2, HD])
        ps = ctx.enter_context(nc.psum_tensor("ps", [P, 8, S], F32))

        smax = [sb(f"smax{k}", [P, 2]) for k in range(2)]
        nmx = [sb(f"nmx{k}", [P, 2]) for k in range(2)]
        den = [sb(f"den{k}", [P, 2]) for k in range(2)]
        sinkd = [sb(f"sinkd{k}", [P, 2]) for k in range(2)]
        sinke = [sb(f"sinke{k}", [P, 2]) for k in range(2)]
        inv = [sb(f"inv{k}", [P, 2]) for k in range(2)]

        with ExitStack() as s:
            ada_acc = [alloc(s, f"ada_acc{k}", [P, D]) for k in range(2)]
            selector = alloc(s, "selector", [33, NDIST])
            rel = alloc(s, "rel", [33, 8])
            relb = alloc(s, "relb", [33, 8, P])
            biasrow = [alloc(s, f"biasrow{k}", [P, NDIST]) for k in range(2)]
        with ExitStack() as s:
            hid_hi, hid_lo = alloc(s, "hid_hi", [P, 8, S], F32R), alloc(s, "hid_lo", [P, 8, S], F32R)
            y = alloc(s, "y", [P, DT, S])
            with ExitStack() as t:
                silu = [alloc(t, f"silu{k}", [P, S]) for k in range(2)]
                prod = [alloc(t, f"prod{k}", [P, S]) for k in range(2)]
            with ExitStack() as t:
                cgate = [alloc(t, f"cgate{k}", [P, S]) for k in range(2)]
                cu = [alloc(t, f"cu{k}", [P, S + 2]) for k in range(2)]
                conv = [alloc(t, f"conv{k}", [P, S]) for k in range(2)]
                bconv = [alloc(t, f"bconv{k}", [P, S]) for k in range(2)]
            with ExitStack() as t:
                q1 = alloc(t, "q1", [P, 8, S])
                k1 = alloc(t, "k1", [P, 2, S])
                v1 = alloc(t, "v1", [P, NT, 256])
                with ExitStack() as r:
                    sig = [alloc(r, f"sig{k}", [P, S]) for k in range(2)]
                    gated = [alloc(r, f"gated{k}", [P, S]) for k in range(2)]
                with ExitStack() as r:
                    unrot = [alloc(r, f"unrot{k}", [P, 2, S]) for k in range(2)]
                    rcos = alloc(r, "rcos", [P, 2, S])
                with ExitStack() as r:
                    sc1 = [alloc(r, f"sc1_{k}", [P, 2, 256]) for k in range(2)]
                    pt1 = [alloc(r, f"pt1_{k}", [P, 2, 256]) for k in range(2)]
        with ExitStack() as s:
            kk = alloc(s, "kk", [P, 2, S])
            vv = alloc(s, "vv", [P, NT, 256])
            nq = alloc(s, "nq", [P, 4, S])
            mqk = alloc(s, "mqk", [P, 4, S])
            mv = alloc(s, "mv", [P, NT, S])
            mo = alloc(s, "mo", [P, 4, S])
            irow, frow = alloc(s, "irow", [P, S]), alloc(s, "frow", [P, S])
            gT = alloc(s, "gT", [P, NT, P])
            kcmp, vcmp = alloc(s, "kcmp", [P, 32]), alloc(s, "vcmp", [32, P])
            with ExitStack() as t:
                kvc, kvs = alloc(t, "kvc", [P, 2, S]), alloc(t, "kvs", [P, 2, S])
                cb = alloc(t, "cb", [P, 16, 62])
                cb_hi = [alloc(t, f"cb_hi{i}", [P, 16, 62], F32R) for i in range(2)]
                cb_lo = [alloc(t, f"cb_lo{i}", [P, 16, 62], F32R) for i in range(2)]
                gsig = alloc(t, "gsig", [P, S])
                with ExitStack() as r:
                    upad = alloc(r, "upad", [P, 2, S + 3])
                    usum = alloc(r, "usum", [P, 2, S])
                with ExitStack() as r:
                    hc = alloc(r, "hc", [64, 2, 256])
                    hcT = alloc(r, "hcT", [P, 2, 2, 62])
            with ExitStack() as t:
                table = alloc(t, "table", [P, 8, S])
                sc2 = [alloc(t, f"sc2_{k}", [P, 2, S]) for k in range(2)]
                pt2 = [alloc(t, f"pt2_{k}", [P, 2, S]) for k in range(2)]
            with ExitStack() as t:
                lfT = alloc(t, "lfT", [P, NT, P])
                aT = alloc(t, "aT", [P, NT, P])
                run = [alloc(t, f"run{k}", [P, S]) for k in range(2)]
                arow = alloc(t, "arow", [P, S])
                emrow = alloc(t, "emrow", [P, S])
                nmax = [alloc(t, f"nmax{k}", [P, S]) for k in range(2)]
                wt = [alloc(t, f"wt{k}", [P, S]) for k in range(2)]
                diag = [alloc(t, f"diag{k}", [P, P]) for k in range(2)]
                drow, dinv = alloc(t, "drow", [P, S]), alloc(t, "dinv", [P, S])
                num = alloc(t, "num", [P, 4, S])
                square4 = [*wt, *nmax]
        with ExitStack() as s:
            alloc(s, "hid_hi_hole", [P, 8, S]), alloc(s, "hid_lo_hole", [P, 8, S])
            alloc(s, "y_hole", [P, DT, S])
            kx = alloc(s, "kx", [P, DT, MEM])
        with ExitStack() as s:
            mn_hi, mn_lo = alloc(s, "mn_hi", [P, DT, MEM], F32R), alloc(s, "mn_lo", [P, DT, MEM], F32R)
            qx = alloc(s, "qx", [P, DT, S])
            alloc(s, "y_hole2", [P, DT, S])
            alloc(s, "kx_hole", [P, DT, MEM])
            vx = alloc(s, "vx", [P, 2, D])
            mt = alloc(s, "mt", [P, DT, MEM])
            mem32 = [alloc(s, f"mem32_{k}", [P, MEM]) for k in range(2)]
            with ExitStack() as t:
                sc3 = [alloc(t, f"sc3_{k}", [P, 2, 256]) for k in range(2)]
                pt3 = [alloc(t, f"pt3_{k}", [P, 2, 256]) for k in range(2)]
        scratch = nc.dram_tensor("bias_rows", (8, P, NDIST), F32, kind="Internal").ap()

        def col(name, i=0, n=1):
            return cols[:, CAT[name] + i:CAT[name] + i + n]

        def const(name, n=None):
            width = dict(CONSTS)[name] if n is None else n
            return consts[:, KAT[name]:KAT[name] + width]

        ident = const("ident")

        x_in, cols_in, consts_in, w2_in = sem("x_in"), sem("cols_in"), sem("consts_in"), sem("w2_in")
        sel_in, rel_in, mem_in = sem("sel_in"), sem("rel_in"), sem("mem_in")
        raw_in = [sem("raw_in0"), sem("raw_in1")]
        split_hi, split_lo = sem("split_hi"), sem("split_lo")
        block_done, block_used = sem("block_done"), sem("block_used")
        ada_step, ada_sum = sem("ada_step"), sem("ada_sum")
        filled, v_step = sem("filled"), sem("v_step")
        c_ready, mods_ready = sem("c_ready"), sem("mods_ready")
        sq_ready, sumsq_step = sem("sq_ready"), sem("sumsq_step")
        ms_ready, root_ready = sem("ms_ready"), sem("root_ready")
        rinv_ready, rstd_ready = sem("rinv_ready"), sem("rstd_ready")
        normed_ready, act32_ready, act_ready = sem("normed_ready"), sem("act32_ready"), sem("act_ready")
        x_ready, mem_hi, mem_ready = sem("x_ready"), sem("mem_hi"), sem("mem_ready")
        silu_ready, hid_ready = sem("silu_ready"), sem("hid_ready")
        relb_ready, brow_sum, brow_copied = sem("relb_ready"), sem("brow_sum"), sem("brow_copied")
        brow_out = [sem("brow_out0"), sem("brow_out1")]
        table_in = sem("table_in")
        cgate_ready, sig_ready, merged_ready = sem("cgate_ready"), sem("sig_ready"), sem("merged_ready")
        merged_hi = sem("merged_hi")
        unrot_ready, rot_sum, rope_done = sem("unrot_ready"), sem("rot_sum"), sem("rope_done")
        scores_ready, biased, negmax_ready = sem("scores_ready"), sem("biased"), sem("negmax_ready")
        exp_done, probs_ready, turned = sem("exp_done"), sem("probs_ready"), sem("turned")
        turned_a, turned_b, pv_done = sem("turned_a"), sem("turned_b"), sem("pv_done")
        out_hi, out_lo = sem("out_hi"), sem("out_lo")
        y_out = sem("y_out")

        heads4 = range(4)
        cp = Steps(sem("cmp_pe"), ["gateT", "swap", "hiddenT", "kcmp", "vcmp"])
        ca = Steps(sem("cmp_act"), ["gsig", "gT", "kvs", "hi0", "hi1", "mq", "mk", "mo0", "mo1",
                                    "hidden0", "hidden1", "hiddenT"])
        cd = Steps(sem("cmp_dve"), ["cb0", "lo0", "cb1", "lo1", "conv0", "conv1", "mk", "kcmp",
                                    "vcmp"])
        mp = Steps(sem("mlstm_pe"), ["lfT", "F", "aT"] + [
            s for h in heads4 for s in [f"max{h}", f"scores{h}0"] + [
                r for kb in range(1, 4) for r in (f"scores{h}{kb}", f"value{h}{kb - 1}")]
            + [f"value{h}3"]] + [f"dinv{h}" for h in heads4] + [f"sum{h}" for h in heads4]
            + [f"rms{h}" for h in heads4])
        ma = Steps(sem("mlstm_act"), ["exp", "ln", "lfT", "aT", "em"] + [
            s for h in heads4 for s in [f"nmax{h}"] + [f"w{h}{kb}" for kb in heads4] + [f"num{h}"]]
            + ["den"] + [f"square{h}" for h in heads4] + ["root"] + [f"hi{h}" for h in heads4])
        md = Steps(sem("mlstm_dve"), ["nabs", "lf", "a", "pos"] + [f"run{i}{e}" for i in range(9)
                                                                for e in "ab"] + ["nem"] + [
            s for h in heads4 for kb in heads4 for s in (f"diag{h}{kb}", f"s{h}{kb}")]
            + ["nden", "floor", "dinv"] + [f"h{h}" for h in heads4] + ["rinv"]
            + [s for h in heads4 for s in (f"n{h}", f"m{h}")])

        items = [("local", j, n, 0) for j in range(8) for n in range(NT)]
        L1 = len(items)
        items += [("sparse", j, n, br) for j in range(4) for n in range(NT) for br in range(3)]
        L2 = len(items)
        items += [("cross", h, pair, 0) for h in range(4) for pair in range(2)]
        L3 = len(items)

        def nkeys(g):
            ph, j, n, br = items[g]
            if ph == "local":
                return 128 if n == 0 else 256
            if ph == "sparse":
                return 8 * n + 7 if br == 0 else 128 * (n + 1)
            return MEM

        def sc(g):
            return {"local": sc1, "sparse": sc2, "cross": sc3}[items[g][0]][g % 2]

        def pt(g):
            return {"local": pt1, "sparse": pt2, "cross": pt3}[items[g][0]][g % 2]

        def key_tiles(g):
            n = nkeys(g)
            return [(k, min(128, n - k)) for k in range(0, n, 128)]

        def out_tiles(g):
            ph, j, n, br = items[g]
            if ph == "local":
                return [(j, 6 + j % 2)] if n == NT - 1 else []
            if ph == "sparse":
                return [(j, 6 + j % 2)] if (n, br) == (NT - 1, 2) else []
            return [(2 * j, 6), (2 * j + 1, 7)] if n == 1 else []

        outs_before = [sum(len(out_tiles(i)) for i in range(g)) for g in range(L3 + 1)]

        def hid_base(ffn, third):
            return ffn * FT + 8 * third + (8 if ffn else 0)

        def scores_of(g):
            return 2 * (g % 2)

        block = ctx.enter_context(nc.Block())

        @block.sync
        def _(sp):
            def load(name, p, k):
                src = ten[name][bass.ds((2 * p + k) * BLOCK, BLOCK)]
                sp.dma_start(raw[k][:].rearrange("p t n -> p (t n)"),
                             src.rearrange("(p n) -> p n", p=P)).then_inc(raw_in[k], 16)

            sp.dma_start(x[:], ten["x"]).then_inc(x_in, 16)
            load("ada", 0, 0)
            load("ada", 0, 1)
            with sp.Fori(1, ADA_BLOCKS // 2) as p:
                for k in range(2):
                    sp.wait_ge(ada_step, 4 * p + 2 * k - 2)
                    load("ada", p, k)
            for k in range(2):
                sp.wait_ge(ada_step, 2 * ADA_BLOCKS - 2 + 2 * k)
                load("weights", 0, k)
            with sp.Fori(1, NB // 2) as p:
                for k in range(2):
                    sp.wait_ge(split_lo, 2 * p + k - 1)
                    load("weights", p, k)
            for t in range(DT):
                sp.wait_ge(x_ready, 3 * DT + t + 1)
                sp.dma_start(ten["out"][:, t, :], x[:, t, :]).then_inc(y_out, 16)
            sp.wait_ge(y_out, 16 * DT)

        @block.tensor
        def _(pe):
            norms = [0]

            def mm(out, lhsT, rhs, start=True, stop=True):
                return nc.tensor.matmul(out, lhsT, rhs, start=start, stop=stop)

            def wait(steps, name):
                pe.wait_ge(steps.sem, steps.at(name))

            def block_fm(p, k, sources, ready=None, tiles=DT, n=S, offset=0):
                b = 2 * p + k
                pe.wait_ge(split_lo, b + 1)
                pe.wait_ge(block_used, b + 1 - offset)
                for t in range(tiles):
                    if ready is not None:
                        pe.wait_ge(ready[0], ready[1] + t + 1)
                    for u in range(2):
                        hi, lo = sources[u]
                        cut = slice(u * P, u * P + P)
                        out = ps[:, 2 * k + u, 0:n]
                        mm(out, w_hi[k][:, t, cut], hi[:, t, 0:n], t == 0, False)
                        mm(out, w_hi[k][:, t, cut], lo[:, t, 0:n], False, False)
                        last = mm(out, w_lo[k][:, t, cut], hi[:, t, 0:n], False, t == tiles - 1)
                last.then_inc(block_done, 1)

            def block_tm(p, k, hi, lo, tokens=NT, offset=0):
                b = 2 * p + k
                pe.wait_ge(split_lo, b + 1)
                pe.wait_ge(block_used, b + 1 - offset)
                for i in range(tokens):
                    out = ps[:, 2 * k + i // 2, (i % 2) * 256:(i % 2) * 256 + 256]
                    cut = slice(i * P, i * P + P)
                    for t in range(DT):
                        mm(out, hi[:, t, cut], w_hi[k][:, t, :], t == 0, False)
                        mm(out, lo[:, t, cut], w_hi[k][:, t, :], False, False)
                        last = mm(out, hi[:, t, cut], w_lo[k][:, t, :], False, t == DT - 1)
                last.then_inc(block_done, 1)

            def stats(blocks=NT):
                nn = norms[0]
                pe.wait_ge(sumsq_step, 7 * (nn + 1))
                for i in range(blocks):
                    last = mm(ps[:, 4, i:i + 1], sumsq[:, i * P:i * P + P], ones[:, 0:1])
                last.then_inc(ms_ready, 1)
                pe.wait_ge(rinv_ready, nn + 1)
                for i in range(blocks):
                    last = mm(ps[:, 5, i * P:i * P + P], rinv[:, i:i + 1].to_broadcast([P, P]), ident)
                last.then_inc(rstd_ready, 1)
                norms[0] += 1

            def ffn(idx, b0, act_base, offset=0):
                src = [(act_hi, act_lo)] * 2
                hid = [(hid_hi, hid_lo)] * 2
                for third, n in enumerate(THIRDS):
                    s = (b0 + 12 * third) // 2
                    with pe.Fori(0, n // 2) as i:
                        for k in range(2):
                            block_fm(s + i, k, src, (act_ready, act_base), offset=offset)
                    s += n // 2
                    with pe.Fori(0, 2) as i:
                        for k in range(2):
                            block_fm(s + i, k, hid, (hid_ready, hid_base(idx, third)), tiles=n,
                                     offset=offset)

            def attention(g0, g1):
                def scores(g):
                    ph, j, n, br = items[g]
                    if g - g0 >= 2:
                        pe.wait_ge(biased, g - 1)
                    nk = nkeys(g)
                    for a in range(2):
                        out = ps[:, scores_of(g) + a, 0:nk]
                        half = slice(64 * a, 64 * a + 64)
                        if ph == "local":
                            k0 = P * (n - 1) if n else 0
                            last = mm(out, q1[half, j, n * P:n * P + P], k1[half, j // 4, k0:k0 + nk])
                        elif ph == "sparse":
                            key = kcmp[half, 0:nk] if br == 0 else kk[half, br - 1, 0:nk]
                            last = mm(out, nq[half, j, n * P:n * P + P], key)
                        else:
                            i = 2 * n + a
                            for e in range(2):
                                last = mm(out, qx[:, 2 * j + e, i * P:i * P + P],
                                          kx[:, 2 * j + e, :], e == 0, e == 1)
                    last.then_inc(scores_ready, 1)

                def turn(g):
                    pe.wait_ge(probs_ready, g + 1)
                    if g > g0:
                        pe.wait_ge(turned_a, g)
                        pe.wait_ge(turned_b, g)
                    for a in range(2):
                        for k, w in key_tiles(g):
                            last = nc.tensor.transpose(ps[0:w, 4 + a, k:k + P], sc(g)[:, a, k:k + w],
                                                       ident)
                    last.then_inc(turned, 1)

                def product(g):
                    ph, j, n, br = items[g]
                    pe.wait_ge(turned_a, g + 1)
                    pe.wait_ge(turned_b, g + 1)
                    if ph == "cross":
                        if n == 0 and j:
                            pe.wait_ge(out_lo, outs_before[g])
                        for a in range(2):
                            m = (2 * n + a) * P
                            for e in range(2):
                                for i in range(2):
                                    f = j * 256 + e * P
                                    last = mm(ps[:, 6 + e, m:m + P], vx[:, i, f:f + P],
                                              pt(g)[:, a, i * P:i * P + P], i == 0, i == 1)
                        last.then_inc(pv_done, 1)
                        return
                    if n == 0 and br == 0 and j >= 2:
                        pe.wait_ge(out_lo, outs_before[g] - 1)
                    tiles = key_tiles(g)
                    for a in range(2):
                        out = ps[64 * a:64 * a + 64, 6 + j % 2, n * P:n * P + P]
                        for i, (k, w) in enumerate(tiles):
                            if ph == "local":
                                f = (j // 4) * P + 64 * a
                                v = v1[:, (n - 1 if n else 0) + i, f:f + 64]
                                start, stop = i == 0, i == len(tiles) - 1
                            elif br == 0:
                                v = vcmp[0:w, 64 * a:64 * a + 64]
                                start, stop = True, False
                            else:
                                f = (br - 1) * P + 64 * a
                                v = vv[:, i, f:f + 64]
                                start, stop = False, br == 2 and i == len(tiles) - 1
                            last = mm(out, v, pt(g)[0:w, a, k:k + P], start, stop)
                    last.then_inc(pv_done, 1)

                scores(g0)
                scores(g0 + 1)
                for g in range(g0, g1):
                    if g + 2 < g1:
                        scores(g + 2)
                    if g > g0:
                        product(g - 1)
                    turn(g)
                product(g1 - 1)

            pe.wait_ge(sel_in, 16)
            pe.wait_ge(relb_ready, 1)
            for h in range(8):
                if h:
                    pe.wait_ge(brow_copied, h)
                mm(ps[:, 2, :], relb[:, h, :], selector[:, 0:S])
                mm(ps[:, 3, 0:NDIST - S], relb[:, h, :], selector[:, S:NDIST]).then_inc(brow_sum, 1)
            for g in range(9):
                pe.wait_ge(ada_step, DT * (g + 1))
                for j in range(DT):
                    last = mm(ps[:, 7, g * DT + j:g * DT + j + 1], ada_acc[g % 2][:, j * P:j * P + P],
                              ones[:, 0:1])
                last.then_inc(ada_sum, 1)
                if g < START:
                    mm(ps[:, 6, 0:1], ones[:], ones[:, 0:1]).then_inc(block_done, 1)
            pe.wait_ge(consts_in, 16)
            stats()
            ffn(0, AT["ffn1"], 0)

            act = [(act_hi, act_lo)] * 2
            stats()
            with pe.Fori(0, 6) as i:
                for k in range(2):
                    block_fm(AT["conv"] // 2 + i, k, act, (act_ready, 8))
            mix = [(act_hi, act_lo), (hid_hi, hid_lo)]
            with pe.Fori(0, 4) as i:
                for k in range(2):
                    block_fm(AT["zconv"] // 2 + i, k, mix, (hid_ready, FT))

            def rotate(r, k):
                pe.wait_ge(unrot_ready, r + 1)
                if r:
                    pe.wait_ge(rope_done, r)
                for u in range(2):
                    last = mm(ps[:, 4 + u, :], const("rot"), unrot[k][:, u, :])
                last.then_inc(rot_sum, 1)

            for r in range(5):
                b = AT["q"] + r
                block_fm(b // 2, b % 2, act)
                if r:
                    rotate(r - 1, (b - 1) % 2)
            block_tm(AT["v"] // 2, 1, act_hi, act_lo)
            rotate(4, 0)
            pe.wait_ge(block_used, used(AT["v"]))
            pe.wait_ge(rope_done, 5)
            attention(0, L1)
            pe.wait_ge(out_lo, outs_before[L1])
            with pe.Fori(0, 4) as i:
                for k in range(2):
                    block_fm(AT["zattn"] // 2 + i, k, mix)
            with pe.Fori(0, 2) as i:
                for k in range(2):
                    block_fm(AT["out1"] // 2 + i, k, act, (act_ready, 16))
            stats()
            ffn(1, AT["ffn2"], 24)

            stats()
            stats()
            block_fm(AT["misc"] // 2, 0, act, (act_ready, 32))
            block_fm(AT["kvc"] // 2, 1, act)
            block_tm(AT["vv"] // 2, 0, act_hi, act_lo)
            wait(ca, "gsig")
            for i in range(NT):
                last = nc.tensor.transpose(ps[:, 6, i * P:i * P + P], gsig[:, i * P:i * P + P], ident)
            last.then_inc(cp.sem, cp.one("gateT"))
            pe.wait_ge(block_used, used(AT["kvc"]))
            for u in range(2):
                last = mm(ps[:, 4 + u, :], const("swap"), kvc[:, u, :])
            last.then_inc(cp.sem, cp.one("swap"))
            block_fm(AT["kk"] // 2, 1, act)
            for b in range(AT["nq"], AT["mv"]):
                block_fm(b // 2, b % 2, act)
            for b in range(AT["mv"], AT["mo"]):
                block_tm(b // 2, b % 2, act_hi, act_lo)
            for b in range(AT["mo"], AT["cmp"]):
                block_fm(b // 2, b % 2, act)
            wait(ca, "kvs")
            for e in range(2):
                wait(cd, f"lo{e}")
                for half in range(2):
                    b = AT["cmp"] + 2 * e + half
                    pe.wait_ge(split_lo, b + 1)
                    for t in range(DT):
                        j, k = 8 * half + t, b % 2
                        out = ps[0:62, 4 + e, 0:256]
                        mm(out, cb_hi[e][:, j, :], w_hi[k][:, t, :], j == 0, False)
                        mm(out, cb_lo[e][:, j, :], w_hi[k][:, t, :], False, False)
                        last = mm(out, cb_hi[e][:, j, :], w_lo[k][:, t, :], False, j == 15)
                    last.then_inc(block_done, 1)
            wait(ca, "hidden1")
            wait(ca, "gT")
            for e in range(2):
                for i in range(2):
                    last = nc.tensor.transpose(ps[:, 6, (2 * e + i) * 64:(2 * e + i) * 64 + 62],
                                               hc[0:62, e, i * P:i * P + P], ident[0:62, 0:62])
            last.then_inc(cp.sem, cp.one("hiddenT"))
            wait(ca, "hiddenT")
            pe.wait_ge(w2_in, 32)
            for a in range(2):
                for i in range(2):
                    last = mm(ps[64 * a:64 * a + 64, 7, 0:31], w2[:, 0, i, :],
                              hcT[:, 0, i, 31 * a:31 * a + 31], i == 0, i == 1)
            last.then_inc(cp.sem, cp.one("kcmp"))
            for a in range(2):
                for i in range(2):
                    last = mm(ps[0:31, 4, 64 * a:64 * a + 64], hcT[:, 1, i, 31 * a:31 * a + 31],
                              w2[:, 1, i, :], i == 0, i == 1)
            last.then_inc(cp.sem, cp.one("vcmp"))
            wait(cd, "vcmp")
            pe.wait_ge(block_used, used(AT["mo"] + 1))
            attention(L1, L2)

            pe.wait_ge(out_lo, outs_before[L2])
            wait(md, "lf")
            for i in range(NT):
                last = nc.tensor.transpose(ps[:, 0, i * P:i * P + P], frow[:, i * P:i * P + P], ident)
            last.then_inc(mp.sem, mp.one("lfT"))
            wait(ma, "lfT")
            for i in range(NT):
                last = mm(ps[:, 1, i * P:S], lfT[:, i, :], const("tri", S - i * P), i == 0, i == NT - 1)
            last.then_inc(mp.sem, mp.one("F"))
            wait(md, "a")
            for i in range(NT):
                last = nc.tensor.transpose(ps[:, 0, i * P:i * P + P], arow[:, i * P:i * P + P], ident)
            last.then_inc(mp.sem, mp.one("aT"))
            wait(md, "run8b")

            def value(h, kb):
                wait(md, f"s{h}{kb}")
                if kb == 0 and h:
                    wait(ma, f"num{h - 1}")
                part = wt[(4 * h + kb) % 2][:, kb * P:S]
                mm(ps[:, 6, kb * P:S], mv[:, kb, h * P:h * P + P], part, kb == 0, kb == 3)
                mm(ps[32 * h:32 * h + 32, 7, kb * P:S], ones[:, 0:32], part, kb == 0, kb == 3) \
                    .then_inc(mp.sem, mp.one(f"value{h}{kb}"))

            for h in heads4:
                row = slice(32 * h, 32 * h + 1)
                half = slice(64 * (h % 2), 64 * (h % 2) + 64)
                if h:
                    wait(ma, f"nmax{h - 1}")
                mm(ps[:, 2, :], ones[row, :], run[1][row, :]).then_inc(mp.sem, mp.one(f"max{h}"))
                for kb in range(NT):
                    c = 4 * h + kb
                    if c >= 2:
                        wait(md, f"s{(c - 2) // 4}{(c - 2) % 4}")
                    mm(ps[:, 4 + c % 2, 0:S - kb * P], mqk[half, 2 + h // 2, kb * P:kb * P + P],
                       mqk[half, h // 2, kb * P:S]).then_inc(mp.sem, mp.one(f"scores{h}{kb}"))
                    if kb:
                        value(h, kb - 1)
                value(h, NT - 1)
            wait(md, "dinv")
            for h in heads4:
                row = slice(32 * h, 32 * h + 1)
                if h >= 2:
                    wait(md, f"h{h - 2}")
                mm(ps[:, h % 2, :], ones[row, :], dinv[row, :]).then_inc(mp.sem, mp.one(f"dinv{h}"))
            for h in heads4:
                wait(ma, f"square{h}")
                mm(ps[32 * h:32 * h + 32, 3, :], ones[:, 0:32], square4[h][:]) \
                    .then_inc(mp.sem, mp.one(f"sum{h}"))
            wait(md, "rinv")
            for h in heads4:
                row = slice(32 * h, 32 * h + 1)
                if h >= 2:
                    wait(md, f"n{h - 2}")
                mm(ps[:, h % 2, :], ones[row, :], dinv[row, :]).then_inc(mp.sem, mp.one(f"rms{h}"))
            wait(md, "m3")

            b = AT["out2"]
            block_fm(b // 2, 0, act, (act_ready, 36), offset=4)
            stats(MEM // P)
            block_fm(b // 2, 1, act, offset=4)
            block_fm(b // 2 + 1, 0, act, offset=4)
            block_fm(b // 2 + 1, 1, act, offset=4)
            memory = [(mn_hi, mn_lo)] * 2
            for q in range(8):
                b = AT["memk"] + q
                if q < 4:
                    block_fm(b // 2, b % 2, memory, (mem_ready, 0), n=MEM, offset=4)
                else:
                    block_tm(b // 2, b % 2, mn_hi, mn_lo, tokens=2, offset=4)
                if q == 0:
                    stats()
                if q == 5:
                    stats()
            with pe.Fori(0, 2) as i:
                for k in range(2):
                    block_fm(AT["xq"] // 2 + i, k, act, (act_ready, 44), offset=4)
            pe.wait_ge(block_used, used(AT["xq"] + 3))
            attention(L2, L3)
            pe.wait_ge(out_lo, outs_before[L3])
            with pe.Fori(0, 2) as i:
                for k in range(2):
                    block_fm(AT["xo"] // 2 + i, k, act, offset=4)
            stats()
            stats()
            ffn(2, AT["ffn3"], 52, offset=4)
            stats()

        @block.scalar
        def _(act):
            norms = [0]
            count = {"normed": 0}

            def fn(out, in_, func=ACT.Copy, **kw):
                return nc.scalar.activation(out, in_, func, **kw)

            def wait(steps, name):
                act.wait_ge(steps.sem, steps.at(name))

            def hi(p, k):
                act.wait_ge(raw_in[k], 16 * (p + ADA_BLOCKS // 2 + 1))
                act.wait_ge(block_done, 2 * p + k + 1)
                fn(w_hi[k][:], raw[k][:]).then_inc(split_hi, 1)

            def hi_next(b):
                if b + 1 < NB:
                    hi((b + 1) // 2, (b + 1) % 2)

            def squares(t, src, n=S):
                nn = norms[0]
                if t == 0:
                    if nn:
                        act.wait_ge(ms_ready, nn)
                    fn(sumsq[:, 0:n], src, ACT.Square).then_inc(sq_ready, 1)
                    return
                if t >= 3 or nn:
                    act.wait_ge(sumsq_step, max(7 * nn, 7 * nn + t - 2))
                fn(square[t % 2][:, 0:n], src, ACT.Square).then_inc(sq_ready, 1)

            def take_root(blocks=NT):
                act.wait_ge(ms_ready, norms[0] + 1)
                fn(root[:, 0:blocks], ps[:, 4, 0:blocks], ACT.Sqrt, bias=eps[:, 0:1],
                   scale=1.0 / D).then_inc(root_ready, 1)
                norms[0] += 1

            def prenorm(shift, gain):
                for t in range(DT):
                    act.wait_ge(normed_ready, count["normed"] + 1)
                    kw = dict(scale=gain[:, t:t + 1])
                    if shift is not None:
                        kw["bias"] = shift[:, t:t + 1]
                    fn(act_hi[:, t, :], normed[t % 2][:], ACT.Identity, **kw)
                    fn(act32[t % 2][:], normed[t % 2][:], ACT.Identity, **kw).then_inc(act32_ready, 1)
                    count["normed"] += 1

            def ffn(b0, source):
                for third, n in enumerate(THIRDS):
                    s = (b0 + 12 * third) // 2
                    with act.Fori(0, n // 2) as i:
                        for k in range(2):
                            hi(s + i + k, 1 - k)
                            act.wait_ge(block_done, 2 * (s + i) + k + START + 1)
                            fn(silu[k][:], ps[:, 2 * k, :], ACT.Silu).then_inc(silu_ready, 1)
                    s += n // 2
                    if third < 2:
                        with act.Fori(0, 2) as i:
                            for k in range(2):
                                hi(s + i + k, 1 - k)
                    else:
                        residual_squares(2 * s, source)

            def residual_squares(b0, source, between=None):
                for q in range(4):
                    b = b0 + q
                    if between is None or q:
                        hi_next(b)
                    if between is not None:
                        between(2 * q)
                        between(2 * q + 1)
                    act.wait_ge(block_used, used(b))
                    for t in (2 * q, 2 * q + 1):
                        squares(t, source[:, t, :])

            def attention(g0, g1):
                def exps(g):
                    act.wait_ge(negmax_ready, g + 1)
                    nk = nkeys(g)
                    for a in range(2):
                        last = fn(sc(g)[:, a, 0:nk], sc(g)[:, a, 0:nk], ACT.Exp,
                                  bias=nmx[g % 2][:, a:a + 1], accum_out=den[g % 2][:, a:a + 1])
                    if items[g][0] == "local":
                        last = fn(sinke[g % 2][:], sinkd[g % 2][:], ACT.Exp)
                    last.then_inc(exp_done, 1)

                def copy_a(g):
                    act.wait_ge(turned, g + 1)
                    if g - g0 >= 2:
                        act.wait_ge(pv_done, g - 1)
                    rows, width = min(nkeys(g), P), P * len(key_tiles(g))
                    fn(pt(g)[0:rows, 0, 0:width], ps[0:rows, 4, 0:width]).then_inc(turned_a, 1)

                def outs(g):
                    target = hid_hi if items[g][0] == "local" else act_hi
                    for t, bank in out_tiles(g):
                        act.wait_ge(pv_done, g + 1)
                        fn(target[:, t, :], ps[:, bank, :]).then_inc(out_hi, 1)

                exps(g0)
                for g in range(g0, g1):
                    if g + 1 < g1:
                        exps(g + 1)
                    copy_a(g)
                    if g > g0:
                        outs(g - 1)
                outs(g1 - 1)

            act.dma_start(cols[:], ten["cols"]).then_inc(cols_in, 16)
            act.dma_start(consts[:], ten["consts"]).then_inc(consts_in, 16)
            act.dma_start(selector[:], ten["selector"]).then_inc(sel_in, 16)
            act.dma_start(rel[0:32, :], ten["rel"]).then_inc(rel_in, 16)
            for e, name in enumerate(("w2k", "w2v")):
                act.dma_start(w2[:, e], ten[name].rearrange("(i p) n -> p i n", p=P)).then_inc(w2_in, 16)
            act.wait_ge(cols_in, 16)
            fn(c_act[:], col("c", 0, DT), ACT.Silu).then_inc(c_ready, 1)
            act.wait_ge(x_in, 16)
            act.wait_ge(filled, 1)
            for t in range(DT):
                squares(t, x[:, t, :])
            for h in range(8):
                act.wait_ge(brow_sum, h + 1)
                if h >= 2:
                    act.wait_ge(brow_out[h % 2], 16 * (h // 2))
                fn(biasrow[h % 2][:], ps[:, 2:4, :].rearrange("p a n -> p (a n)")[:, 0:NDIST]) \
                    .then_inc(brow_copied, 1)
                act.wait_ge(brow_copied, h + 1)
                act.dma_start(scratch[h], biasrow[h % 2][:]).then_inc(brow_out[h % 2], 16)
            take_root()
            hi(0, 0)
            act.wait_ge(mods_ready, 1)
            for k in range(2):
                act.wait_ge(brow_out[k], 64)
            prenorm(mods[:, 0:8], gains[:, 0])
            ffn(AT["ffn1"], x)

            take_root()
            prenorm(mods[:, 24:32], gains[:, 1])
            for i in range(4):
                for u in range(2):
                    b = AT["conv"] + 3 * i + u
                    hi_next(b)
                    act.wait_ge(block_done, done(b))
                    fn(cgate[u][:], ps[:, 2 * (b % 2), :]).then_inc(cgate_ready, 1)
                hi_next(b + 1)

            def gates(b0):
                with act.Fori(0, 4) as i:
                    for k in range(2):
                        hi(b0 // 2 + i + k, 1 - k)
                        act.wait_ge(block_done, 2 * i + b0 + k + START + 1)
                        fn(sig[k][:], ps[:, 2 * k, :], ACT.Sigmoid).then_inc(sig_ready, 1)

            gates(AT["zconv"])
            for r in range(5):
                b = AT["q"] + r
                hi_next(b)
                act.wait_ge(block_done, done(b))
                if r == 0:
                    act.wait_ge(block_used, used(b - 1))
                if r >= 2:
                    act.wait_ge(rot_sum, r - 1)
                fn(unrot[b % 2][:], ps[:, 2 * (b % 2):2 * (b % 2) + 2, :],
                   scale=HD ** -0.5 if r < 4 else 1.0).then_inc(unrot_ready, 1)
            hi_next(AT["v"])
            attention(0, L1)
            gates(AT["zattn"])
            act.wait_ge(block_done, done(AT["out1"] - 1))
            for t in range(DT):
                act.wait_ge(merged_ready, t + 1)
                fn(act_hi[:, t, :], y[:, t, :]).then_inc(merged_hi, 1)
            residual_squares(AT["out1"], x)
            take_root()
            prenorm(mods[:, 48:56], gains[:, 2])
            ffn(AT["ffn2"], x)

            take_root()
            for t in range(DT):
                act.wait_ge(x_ready, t + 1)
                squares(t, x[:, t, :])
            take_root()
            prenorm(None, col("mixpre", 0, DT))
            b = AT["misc"]
            hi_next(b)
            act.wait_ge(block_used, used(b))
            fn(gsig[:], irow[:], ACT.Sigmoid).then_inc(ca.sem, ca.one("gsig"))
            hi_next(AT["kvc"])
            hi_next(AT["vv"])
            wait(cp, "gateT")
            fn(gT[:], ps[:, 6, :].rearrange("p (i n) -> p i n", n=P)).then_inc(ca.sem, ca.one("gT"))
            wait(cp, "swap")
            fn(kvs[:], ps[:, 4:6, :]).then_inc(ca.sem, ca.one("kvs"))
            hi_next(AT["kk"])
            for e in range(2):
                hi_next(AT["nq"] + e)
                wait(cd, f"cb{e}")
                fn(cb_hi[e][:], cb[:]).then_inc(ca.sem, ca.one(f"hi{e}"))
            for e, name in enumerate(("mq", "mk")):
                hi_next(AT[name])
                wait(cd, f"conv{e}")
                for u in range(2):
                    last = fn(mqk[:, 2 * e + u, :], usum[:, u, :], ACT.Silu,
                              bias=col("conv2b", 2 * e + u))
                last.then_inc(ca.sem, ca.one(name))
            hi_next(AT["mv"])
            hi_next(AT["mv"] + 1)
            for e in range(2):
                hi_next(AT["mo"] + e)
                act.wait_ge(block_used, used(AT["mo"] + e))
                fn(mo[:, 2 * e:2 * e + 2, :], mo[:, 2 * e:2 * e + 2, :], ACT.Sigmoid) \
                    .then_inc(ca.sem, ca.one(f"mo{e}"))
            for e in range(2):
                hi_next(AT["cmp"] + 2 * e)
                hi_next(AT["cmp"] + 2 * e + 1)
                act.wait_ge(block_done, done(AT["cmp"] + 2 * e + 1))
                fn(hc[0:62, e, :], ps[0:62, 4 + e, 0:256], ACT.Silu) \
                    .then_inc(ca.sem, ca.one(f"hidden{e}"))
            wait(cp, "hiddenT")
            fn(hcT[:].rearrange("p e i n -> p (e i) n"),
               ps[:, 6, 0:256].rearrange("p (a n) -> p a n", n=64)[:, :, 0:62]) \
                .then_inc(ca.sem, ca.one("hiddenT"))
            wait(cd, "vcmp")
            wait(cp, "vcmp")
            for h in range(8):
                row = scratch[h].rearrange("p n -> (p n)")
                skew = row[P - 1:P - 1 + P * (NDIST - 1)].rearrange("(p n) -> p n", n=NDIST - 1)
                act.dma_start(table[:, h, :], skew[:, 0:S]).then_inc(table_in, 16)
            attention(L1, L2)

            wait(md, "nabs")
            fn(run[1][:], run[0][:], ACT.Exp).then_inc(ma.sem, ma.one("exp"))
            wait(ma, "exp")
            fn(arow[:], run[1][:], ACT.Ln, bias=ones[:, 0:1]).then_inc(ma.sem, ma.one("ln"))
            wait(mp, "lfT")
            fn(lfT[:], ps[:, 0, :].rearrange("p (i n) -> p i n", n=P)).then_inc(ma.sem, ma.one("lfT"))
            wait(mp, "aT")
            fn(aT[:], ps[:, 0, :].rearrange("p (i n) -> p i n", n=P)).then_inc(ma.sem, ma.one("aT"))
            wait(md, "nem")
            fn(emrow[:], emrow[:], ACT.Exp).then_inc(ma.sem, ma.one("em"))
            wait(ma, "aT")
            for h in heads4:
                wait(mp, f"max{h}")
                if h >= 2:
                    wait(md, f"diag{h - 2}3")
                    wait(ma, f"w{h - 2}3")
                fn(nmax[h % 2][:], ps[:, 2, :], scale=-1.0).then_inc(ma.sem, ma.one(f"nmax{h}"))
                wait(ma, f"nmax{h}")
                for kb in range(NT):
                    c, t0 = 4 * h + kb, kb * P
                    wait(md, f"diag{h}{kb}")
                    if c >= 2:
                        wait(mp, f"value{(c - 2) // 4}{(c - 2) % 4}")
                    a = aT[:, kb, 32 * h:32 * h + 1]
                    last = fn(wt[c % 2][:, t0:t0 + P], diag[c % 2][:], ACT.Exp, bias=a)
                    if kb < NT - 1:
                        last = fn(wt[c % 2][:, t0 + P:S], nmax[h % 2][:, t0 + P:S], ACT.Exp, bias=a)
                    last.then_inc(ma.sem, ma.one(f"w{h}{kb}"))
                wait(mp, f"value{h}3")
                fn(num[:, h, :], ps[:, 6, :]).then_inc(ma.sem, ma.one(f"num{h}"))
            fn(drow[:], ps[:, 7, :]).then_inc(ma.sem, ma.one("den"))
            for h in heads4:
                wait(md, f"h{h}")
                fn(square4[h][:], num[:, h, :], ACT.Square).then_inc(ma.sem, ma.one(f"square{h}"))
            wait(mp, "sum3")
            fn(drow[:], ps[:, 3, :], ACT.Sqrt, bias=eps[:, 0:1], scale=1.0 / P) \
                .then_inc(ma.sem, ma.one("root"))
            for h in heads4:
                wait(md, f"m{h}")
                fn(act_hi[:, 4 + h, :], num[:, h, :]).then_inc(ma.sem, ma.one(f"hi{h}"))

            act.wait_ge(act_ready, 44)
            act.dma_start(mt[:], ten["mem"]).then_inc(mem_in, 16)
            act.wait_ge(mem_in, 16)
            for t in range(DT):
                squares(t, mt[:, t, :], MEM)
            hi_next(AT["out2"])
            take_root(MEM // P)

            def memory_high(t):
                act.wait_ge(normed_ready, count["normed"] + 1)
                fn(mn_hi[:, t, :], mem32[t % 2][:]).then_inc(mem_hi, 1)
                count["normed"] += 1

            residual_squares(AT["out2"], y, between=memory_high)
            hi_next(AT["memk"])
            take_root()
            for q in range(1, 8):
                hi_next(AT["memk"] + q)
                if 1 <= q <= 4:
                    for t in (2 * q - 2, 2 * q - 1):
                        act.wait_ge(x_ready, DT + t + 1)
                        squares(t, x[:, t, :])
                if q == 5:
                    take_root()
            prenorm(None, col("xpre", 0, DT))
            for q in range(4):
                hi_next(AT["xq"] + q)
            attention(L2, L3)
            residual_squares(AT["xo"], y)
            take_root()
            for t in range(DT):
                act.wait_ge(x_ready, 2 * DT + t + 1)
                squares(t, x[:, t, :])
            take_root()
            prenorm(None, col("fpre", 0, DT))
            ffn(AT["ffn3"], y)
            take_root()

        @block.vector
        def _(dve):
            norms = [0]
            count = {"step": 0, "act32": 0, "silu": 0}
            v = nc.vector

            def wait(steps, name):
                dve.wait_ge(steps.sem, steps.at(name))

            def link(ins):
                ins.then_inc(v_step, 1)
                count["step"] += 1
                dve.wait_ge(v_step, count["step"])

            def lo(p, k):
                dve.wait_ge(split_hi, 2 * p + k + 1)
                v.tensor_tensor(w_lo[k][:], raw[k][:], w_hi[k][:].bitcast(F32),
                                ALU.subtract).then_inc(split_lo, 1)

            def lo_next(b):
                if b + 1 < NB:
                    lo((b + 1) // 2, (b + 1) % 2)

            def banks(b):
                return ps[:, 2 * (b % 2):2 * (b % 2) + 2, :]

            def add_squares(t, n=S):
                nn = norms[0]
                if t == 0:
                    return
                dve.wait_ge(sq_ready, DT * nn + t + 1)
                if t > 1:
                    dve.wait_ge(sumsq_step, 7 * nn + t - 1)
                v.tensor_tensor(sumsq[:, 0:n], sumsq[:, 0:n], square[t % 2][:, 0:n],
                                ALU.add).then_inc(sumsq_step, 1)

            def invert(blocks=NT):
                dve.wait_ge(root_ready, norms[0] + 1)
                v.reciprocal(rinv[:, 0:blocks], root[:, 0:blocks]).then_inc(rinv_ready, 1)
                dve.wait_ge(rstd_ready, norms[0] + 1)
                norms[0] += 1

            def prenorm():
                def low(t):
                    dve.wait_ge(act32_ready, count["act32"] - DT + t + 1)
                    v.tensor_tensor(act_lo[:, t, :], act32[t % 2][:], act_hi[:, t, :].bitcast(F32),
                                    ALU.subtract).then_inc(act_ready, 1)

                count["act32"] += DT
                for t in range(DT):
                    if t >= 2:
                        low(t - 2)
                    v.tensor_tensor(normed[t % 2][:], x[:, t, :], ps[:, 5, :],
                                    ALU.mult).then_inc(normed_ready, 1)
                low(DT - 2)
                low(DT - 1)

            def post(t, name):
                link(v.scalar_tensor_tensor(out=normed[t % 2][:], in0=y[:, t, :], scalar=col(name, t),
                                            in1=ps[:, 5, :], op0=ALU.mult, op1=ALU.mult))
                v.tensor_tensor(x[:, t, :], x[:, t, :], normed[t % 2][:],
                                ALU.add).then_inc(x_ready, 1)

            def tiles2(ap, m):
                return ap[:, m:m + 2, :] if isinstance(m, int) else ap[:, bass.ds(m, 2), :]

            def update(p, k, m, gate, third):
                dve.wait_ge(block_done, 2 * p + k + START + 1)
                if gate is None:
                    out, sums = tiles2(y, m), ps[:, 2 * k:2 * k + 2, :]
                    if third == 0:
                        v.tensor_copy(out, sums).then_inc(block_used, 1)
                    else:
                        v.tensor_tensor(out, out, sums, ALU.add).then_inc(block_used, 1)
                    return
                for u in range(2):
                    at = slice(m + u, m + u + 1) if isinstance(m, int) else bass.ds(m + u, 1)
                    tile = x[:, at, :].rearrange("p a n -> p (a n)")
                    last = v.scalar_tensor_tensor(out=tile, in0=ps[:, 2 * k + u, :],
                                                  scalar=gate[:, at], in1=tile,
                                                  op0=ALU.mult, op1=ALU.add)
                last.then_inc(block_used, 1)

            def final_updates(b0, gate, third=2, between=None):
                for q in range(4):
                    b = b0 + q
                    if between is None or q:
                        lo_next(b)
                    if between is not None:
                        between(2 * q)
                        between(2 * q + 1)
                    update(b // 2, b % 2, 2 * q, gate, third)
                    add_squares(2 * q)
                    add_squares(2 * q + 1)

            def ffn(b0, gate):
                offset = 4 if gate is None else 0
                for third, n in enumerate(THIRDS):
                    s = (b0 + 12 * third) // 2
                    per = 2
                    with dve.Fori(0, n // 2) as i:
                        for k in range(2):
                            b = 2 * (s + i) + k
                            lo(s + i + k, 1 - k)
                            dve.wait_ge(silu_ready, count["silu"] + 2 * i + k + 1)
                            v.tensor_tensor(prod[k][:], silu[k][:], ps[:, 2 * k + 1, :],
                                            ALU.mult).then_inc(block_used, 1)
                            dve.wait_ge(block_used, b + START + 1 - offset)
                            at = bass.ds(2 * i + k, 1)
                            hi_tile = hid_hi[:, at, :].rearrange("p a n -> p (a n)")
                            lo_tile = hid_lo[:, at, :].rearrange("p a n -> p (a n)")
                            v.tensor_scalar(hi_tile, prod[k][:], 1.0, None,
                                            ALU.mult).then_inc(v_step, 1)
                            dve.wait_ge(v_step, count["step"] + per * i + k + 1)
                            v.tensor_tensor(lo_tile, prod[k][:], hi_tile.bitcast(F32),
                                            ALU.subtract).then_inc(hid_ready, 1)
                    count["step"] += per * (n // 2)
                    count["silu"] += n
                    s += n // 2
                    if third < 2:
                        with dve.Fori(0, 2) as i:
                            for k in range(2):
                                lo(s + i + k, 1 - k)
                                update(s + i, k, 4 * i + 2 * k, gate, third)
                    else:
                        final_updates(2 * s, gate)

            def attention(g0, g1):
                def bias(g):
                    ph, j, n, br = items[g]
                    nk = nkeys(g)
                    dve.wait_ge(scores_ready, g + 1)
                    if g - g0 >= 2:
                        dve.wait_ge(turned, g - 1)
                    for a in range(2):
                        if ph == "local":
                            add = const("mask")[:, 256 - nk:256]
                        elif ph == "sparse":
                            first = P * (NT - 1 - n)
                            row = table[:, j + 4 * a, :]
                            add = row[:, first + 31:S:16] if br == 0 else row[:, first:S]
                        else:
                            add = zeros[:, 0:nk]
                        last = v.tensor_tensor_reduce(sc(g)[:, a, 0:nk],
                                                      ps[:, scores_of(g) + a, 0:nk], add, 1.0, -3e38,
                                                      ALU.add, ALU.max, smax[g % 2][:, a:a + 1])
                    last.then_inc(biased, 1)
                    dve.wait_ge(biased, g + 1)
                    if ph == "local":
                        sink = negsink[:, 2 * j:2 * j + 2]
                        link(v.scalar_tensor_tensor(out=nmx[g % 2][:], in0=smax[g % 2][:], scalar=-1.0,
                                                    in1=sink, op0=ALU.mult, op1=ALU.min))
                        v.tensor_tensor(sinkd[g % 2][:], nmx[g % 2][:], sink,
                                        ALU.subtract).then_inc(negmax_ready, 1)
                    else:
                        v.tensor_scalar(nmx[g % 2][:], smax[g % 2][:], -1.0, None,
                                        ALU.mult).then_inc(negmax_ready, 1)

                def norm(g):
                    ph, j, n, br = items[g]
                    dve.wait_ge(exp_done, g + 1)
                    total, w = den[g % 2], inv[g % 2]
                    if ph == "local":
                        link(v.tensor_tensor(total[:], total[:], sinke[g % 2][:], ALU.add))
                    link(v.reciprocal(w[:], total[:]))
                    if ph == "sparse":
                        gate = gT[:, n, 1 + 3 * j + br:14 + 3 * j + br:12]
                        if n == 0 and br == 0:
                            link(v.scalar_tensor_tensor(out=w[:], in0=w[:], scalar=const("valid"),
                                                        in1=gate, op0=ALU.mult, op1=ALU.mult))
                        else:
                            link(v.tensor_tensor(w[:], w[:], gate, ALU.mult))
                    nk = nkeys(g)
                    for a in range(2):
                        last = v.tensor_scalar(sc(g)[:, a, 0:nk], sc(g)[:, a, 0:nk], w[:, a:a + 1],
                                               None, ALU.mult)
                    last.then_inc(probs_ready, 1)

                def copy_b(g):
                    dve.wait_ge(turned, g + 1)
                    if g - g0 >= 2:
                        dve.wait_ge(pv_done, g - 1)
                    rows, width = min(nkeys(g), P), P * len(key_tiles(g))
                    v.tensor_copy(pt(g)[0:rows, 1, 0:width],
                                  ps[0:rows, 5, 0:width]).then_inc(turned_b, 1)

                def outs(g):
                    hi_to, lo_to = (hid_hi, hid_lo) if items[g][0] == "local" else (act_hi, act_lo)
                    for i, (t, bank) in enumerate(out_tiles(g)):
                        dve.wait_ge(out_hi, outs_before[g] + i + 1)
                        v.tensor_tensor(lo_to[:, t, :], ps[:, bank, :], hi_to[:, t, :].bitcast(F32),
                                        ALU.subtract).then_inc(out_lo, 1)

                bias(g0)
                for g in range(g0, g1):
                    if g + 1 < g1:
                        bias(g + 1)
                    norm(g)
                    if g > g0:
                        copy_b(g - 1)
                    if g > g0 + 1:
                        outs(g - 2)
                copy_b(g1 - 1)
                outs(g1 - 2)
                outs(g1 - 1)

            v.memset(ones[:], 1.0)
            v.memset(zeros[:], 0.0)
            v.memset(eps[:], EPS).then_inc(filled, 1)
            dve.wait_ge(filled, 1)
            dve.wait_ge(rel_in, 16)
            link(v.memset(rel[32:33, :], 1.0))
            for h in range(8):
                last = v.tensor_scalar(relb[:, h, :], ones[0:33, :], rel[:, h:h + 1], None, ALU.mult)
            last.then_inc(relb_ready, 1)
            for t in range(DT):
                add_squares(t)
            for k in range(START):
                v.memset(nmx[k][:], 0.0).then_inc(block_used, 1)
            dve.wait_ge(c_ready, 1)

            def ada_group(g, acc, p0):
                for i in range(4):
                    dve.wait_ge(raw_in[i % 2], 16 * (p0 + i // 2 + 1))
                    for u in range(2):
                        t = 2 * i + u
                        w = raw[i % 2][:].rearrange("p t n -> p (t n)")[:, u * D:u * D + D]
                        if t == 0:
                            ins = v.tensor_scalar(acc[:], w, c_act[:, 0:1], None, ALU.mult)
                        else:
                            dve.wait_ge(ada_step, DT * g + t)
                            ins = v.scalar_tensor_tensor(out=acc[:], in0=w, scalar=c_act[:, t:t + 1],
                                                         in1=acc[:], op0=ALU.mult, op1=ALU.add)
                        ins.then_inc(ada_step, 1)

            for g in range(3):
                if g == 2:
                    dve.wait_ge(ada_sum, 1)
                ada_group(g, ada_acc[g % 2], 2 * g)
            with dve.Fori(0, 3) as i:
                for u in range(2):
                    dve.wait_ge(ada_sum, 2 * i + u + 2)
                    ada_group(2 * i + u + 3, ada_acc[(u + 1) % 2], 4 * i + 2 * u + 6)
            dve.wait_ge(ada_sum, 9)
            link(v.tensor_tensor(mods[:], ps[:, 7, 0:72], col("b_ada", 0, 72), ALU.add))
            for i, (scale, name) in enumerate(((1, "g_ffn1"), (4, "g_mix"), (7, "g_ffn2"))):
                v.scalar_tensor_tensor(out=gains[:, i, :], in0=mods[:, 8 * scale:8 * scale + 8],
                                       scalar=1.0, in1=col(name, 0, DT), op0=ALU.add, op1=ALU.mult)
            v.tensor_scalar(gains[:, 3, :], mods[:, 16:24], 0.5, None, ALU.mult)
            v.tensor_scalar(gains[:, 4, :], mods[:, 64:72], 0.5, None, ALU.mult)
            v.tensor_scalar(negsink[:], col("sinks", 0, 16), -1.0, None, ALU.mult) \
                .then_inc(mods_ready, 1)
            dve.wait_ge(mods_ready, 1)
            invert()
            prenorm()
            lo(0, 0)
            ffn(AT["ffn1"], gains[:, 3])

            invert()
            prenorm()
            for u in range(2):
                last = v.memset(cu[u][:, 0:2], 0.0)
            link(last)
            for i in range(4):
                for u in range(2):
                    b = AT["conv"] + 3 * i + u
                    lo_next(b)
                    dve.wait_ge(cgate_ready, 2 * i + u + 1)
                    v.tensor_tensor(cu[u][:, 2:], cgate[u][:], ps[:, 2 * (b % 2) + 1, :],
                                    ALU.mult).then_inc(block_used, 1)
                    dve.wait_ge(block_used, used(b))
                    j = 2 * i + u
                    link(v.tensor_scalar(conv[u][:], cu[u][:, 0:S], col("conv", j), None, ALU.mult))
                    for tap in (1, 2):
                        link(v.scalar_tensor_tensor(out=conv[u][:], in0=cu[u][:, tap:tap + S],
                                                    scalar=col("conv", 8 * tap + j), in1=conv[u][:],
                                                    op0=ALU.mult, op1=ALU.add))
                b = AT["conv"] + 3 * i + 2
                lo_next(b)
                dve.wait_ge(block_done, done(b))
                for u in range(2):
                    last = v.tensor_tensor(bconv[u][:], conv[u][:], ps[:, 2 * (b % 2) + u, :], ALU.mult)
                last.then_inc(block_used, 1)
                dve.wait_ge(block_used, used(b))
                for u in range(2):
                    link(v.tensor_scalar(hid_hi[:, 2 * i + u, :], bconv[u][:], 1.0, None, ALU.mult))
                    v.tensor_tensor(hid_lo[:, 2 * i + u, :], bconv[u][:],
                                    hid_hi[:, 2 * i + u, :].bitcast(F32),
                                    ALU.subtract).then_inc(hid_ready, 1)
            with dve.Fori(0, 4) as i:
                for k in range(2):
                    lo(AT["zconv"] // 2 + i + k, 1 - k)
                    dve.wait_ge(sig_ready, 2 * i + k + 1)
                    tile = y[:, bass.ds(2 * i + k, 1), :].rearrange("p a n -> p (a n)")
                    v.tensor_tensor(tile, sig[k][:], ps[:, 2 * k + 1, :],
                                    ALU.mult).then_inc(block_used, 1)

            def rope(r, b):
                out = q1[:, 2 * r:2 * r + 2, :] if r < 4 else k1[:]
                dve.wait_ge(rot_sum, r + 1)
                sin = const("sin").unsqueeze(1).to_broadcast([P, 2, S])
                link(v.tensor_tensor(out, ps[:, 4:6, :], sin, ALU.mult))
                v.tensor_tensor(out, out, rcos[:], ALU.add).then_inc(rope_done, 1)

            for r in range(5):
                b = AT["q"] + r
                lo_next(b)
                if r:
                    rope(r - 1, b - 1)
                dve.wait_ge(unrot_ready, r + 1)
                if r:
                    dve.wait_ge(rope_done, r)
                cos = const("cos").unsqueeze(1).to_broadcast([P, 2, S])
                v.tensor_tensor(rcos[:], unrot[b % 2][:], cos, ALU.mult).then_inc(block_used, 1)
                dve.wait_ge(block_used, used(b))
            b = AT["v"]
            lo_next(b)
            dve.wait_ge(block_done, done(b))
            v.tensor_copy(v1[:].rearrange("p i n -> p (i n)"),
                          banks(b).rearrange("p a n -> p (a n)")).then_inc(block_used, 1)
            rope(4, b - 1)
            attention(0, L1)
            with dve.Fori(0, 4) as i:
                for k in range(2):
                    b = AT["zattn"] + 2 * i + k
                    lo(AT["zattn"] // 2 + i + k, 1 - k)
                    dve.wait_ge(sig_ready, 8 + 2 * i + k + 1)
                    v.tensor_tensor(gated[k][:], sig[k][:], ps[:, 2 * k + 1, :],
                                    ALU.mult).then_inc(block_used, 1)
                    dve.wait_ge(block_used, b + START + 1)
                    tile = y[:, bass.ds(2 * i + k, 1), :].rearrange("p a n -> p (a n)")
                    v.tensor_tensor(tile, tile, gated[k][:], ALU.add).then_inc(merged_ready, 1)
            for t in range(DT):
                dve.wait_ge(merged_hi, t + 1)
                v.tensor_tensor(act_lo[:, t, :], y[:, t, :], act_hi[:, t, :].bitcast(F32),
                                ALU.subtract).then_inc(act_ready, 1)
            final_updates(AT["out1"], mods[:, 40:48])
            invert()
            prenorm()
            ffn(AT["ffn2"], gains[:, 4])

            invert()
            for t in range(DT):
                v.scalar_tensor_tensor(out=x[:, t, :], in0=x[:, t, :], scalar=col("g_final", t),
                                       in1=ps[:, 5, :], op0=ALU.mult,
                                       op1=ALU.mult).then_inc(x_ready, 1)
            for t in range(DT):
                add_squares(t)
            invert()
            prenorm()
            link(v.memset(upad[:, :, 0:3], 0.0))
            b = AT["misc"]
            lo_next(b)
            dve.wait_ge(block_done, done(b))
            v.tensor_scalar(irow[:], ps[:, 0, :], col("gate_bias", 0), None, ALU.add)
            v.tensor_scalar(frow[:], ps[:, 1, :], col("gate_bias", 1), None,
                            ALU.add).then_inc(block_used, 1)

            def take(b, out, scale=None):
                lo_next(b)
                dve.wait_ge(block_done, done(b))
                if scale is None:
                    ins = v.tensor_copy(out, banks(b))
                else:
                    ins = v.tensor_scalar(out, banks(b), scale, None, ALU.mult)
                ins.then_inc(block_used, 1)

            def quarters(b):
                return banks(b).rearrange("p a (c n) -> p (a c) n", n=256)

            take(AT["kvc"], kvc[:])
            b = AT["vv"]
            lo_next(b)
            dve.wait_ge(block_done, done(b))
            v.tensor_copy(vv[:], quarters(b)).then_inc(block_used, 1)
            take(AT["kk"], kk[:])
            for e in range(2):
                take(AT["nq"] + e, nq[:, 2 * e:2 * e + 2, :], HD ** -0.5)
                if e == 0:
                    wait(ca, "kvs")
                else:
                    wait(cd, "lo0")
                for parity in range(2):
                    half = slice(64 * parity, 64 * parity + 64)
                    for a in range(2):
                        src = (kvc if a == parity else kvs)[half, e, :] \
                            .rearrange("p (c j s) -> p j c s", j=8, s=2)
                        for up in range(2):
                            pos = col("pos_k" if e == 0 else "pos_v", 8 * up, 8)[half, :]
                            last = v.tensor_tensor(
                                cb[half, 8 * up:8 * up + 8, 31 * a:31 * a + 31],
                                src[:, :, up:up + 31, parity],
                                pos.unsqueeze(2).to_broadcast([64, 8, 31]), ALU.add)
                last.then_inc(cd.sem, cd.one(f"cb{e}"))
                wait(ca, f"hi{e}")
                v.tensor_tensor(cb_lo[e][:], cb[:], cb_hi[e][:].bitcast(F32),
                                ALU.subtract).then_inc(cd.sem, cd.one(f"lo{e}"))
            for e, name in enumerate(("mq", "mk")):
                take(AT[name], upad[:, :, 3:])
                dve.wait_ge(block_used, used(AT[name]))
                if e:
                    wait(ca, "mq")
                for u in range(2):
                    j = 2 * e + u
                    link(v.tensor_scalar(usum[:, u, :], upad[:, u, 0:S], col("conv2", j), None,
                                         ALU.mult))
                    for tap in (1, 2, 3):
                        ins = v.scalar_tensor_tensor(out=usum[:, u, :], in0=upad[:, u, tap:tap + S],
                                                     scalar=col("conv2", 4 * tap + j),
                                                     in1=usum[:, u, :], op0=ALU.mult, op1=ALU.add)
                        if u == 1 and tap == 3:
                            ins.then_inc(cd.sem, cd.one(f"conv{e}"))
                        else:
                            link(ins)
            for e in range(2):
                b = AT["mv"] + e
                lo_next(b)
                dve.wait_ge(block_done, done(b))
                v.tensor_copy(mv[:, :, 256 * e:256 * e + 256], quarters(b)).then_inc(block_used, 1)
            wait(ca, "mk")
            v.tensor_scalar(mqk[:, 2:4, :], mqk[:, 2:4, :], HD ** -0.5, None,
                            ALU.mult).then_inc(cd.sem, cd.one("mk"))
            for e in range(2):
                take(AT["mo"] + e, mo[:, 2 * e:2 * e + 2, :])
            for b in range(AT["cmp"], AT["cmp"] + 4):
                lo_next(b)
            wait(cp, "kcmp")
            v.tensor_copy(kcmp[:, 0:31], ps[:, 7, 0:31]).then_inc(cd.sem, cd.one("kcmp"))
            wait(cp, "vcmp")
            v.tensor_copy(vcmp[0:31, :], ps[0:31, 4, 0:P]).then_inc(cd.sem, cd.one("vcmp"))
            dve.wait_ge(table_in, 16 * 8)
            attention(L1, L2)

            v.scalar_tensor_tensor(out=run[0][:], in0=frow[:], scalar=-1.0, in1=frow[:],
                                   op0=ALU.mult, op1=ALU.min).then_inc(md.sem, md.one("nabs"))
            wait(ma, "ln")
            v.scalar_tensor_tensor(out=frow[:], in0=frow[:], scalar=0.0, in1=arow[:],
                                   op0=ALU.min, op1=ALU.subtract).then_inc(md.sem, md.one("lf"))
            wait(mp, "F")
            v.tensor_tensor(arow[:], irow[:], ps[:, 1, :], ALU.subtract) \
                .then_inc(md.sem, md.one("a"))
            wait(md, "a")
            v.tensor_scalar(run[0][:], arow[:], 0.0, None, ALU.max).then_inc(md.sem, md.one("pos"))
            wait(md, "pos")
            for i in range(9):
                src, dst, w = run[i % 2], run[1 - i % 2], 1 << i
                v.tensor_copy(dst[:, 0:w], src[:, 0:w]).then_inc(md.sem, md.one(f"run{i}a"))
                v.tensor_tensor(dst[:, w:], src[:, w:], src[:, 0:S - w], ALU.max) \
                    .then_inc(md.sem, md.one(f"run{i}b"))
                wait(md, f"run{i}b")
            v.scalar_tensor_tensor(out=emrow[:], in0=run[1][:], scalar=-1.0, in1=ps[:, 1, :],
                                   op0=ALU.mult, op1=ALU.subtract).then_inc(md.sem, md.one("nem"))
            for h in heads4:
                wait(ma, f"nmax{h}")
                for kb in range(NT):
                    c, t0 = 4 * h + kb, kb * P
                    if c >= 2:
                        wait(ma, f"w{(c - 2) // 4}{(c - 2) % 4}")
                    v.tensor_tensor(diag[c % 2][:], nmax[h % 2][:, t0:t0 + P], const("maskT"),
                                    ALU.add).then_inc(md.sem, md.one(f"diag{h}{kb}"))
                    wait(mp, f"scores{h}{kb}")
                    wait(ma, f"w{h}{kb}")
                    v.tensor_tensor(wt[c % 2][:, t0:S], ps[:, 4 + c % 2, 0:S - t0], wt[c % 2][:, t0:S],
                                    ALU.mult).then_inc(md.sem, md.one(f"s{h}{kb}"))
            wait(ma, "den")
            v.scalar_tensor_tensor(out=dinv[:], in0=drow[:], scalar=-1.0, in1=drow[:],
                                   op0=ALU.mult, op1=ALU.max).then_inc(md.sem, md.one("nden"))
            wait(md, "nden")
            wait(ma, "em")
            v.tensor_tensor(dinv[:], dinv[:], emrow[:], ALU.max).then_inc(md.sem, md.one("floor"))
            wait(md, "floor")
            v.reciprocal(dinv[:], dinv[:]).then_inc(md.sem, md.one("dinv"))
            for h in heads4:
                wait(mp, f"dinv{h}")
                v.tensor_tensor(num[:, h, :], num[:, h, :], ps[:, h % 2, :], ALU.mult) \
                    .then_inc(md.sem, md.one(f"h{h}"))
            wait(ma, "root")
            v.reciprocal(dinv[:], drow[:]).then_inc(md.sem, md.one("rinv"))

            def mlstm_low(h):
                wait(ma, f"hi{h}")
                v.tensor_tensor(act_lo[:, 4 + h, :], num[:, h, :], act_hi[:, 4 + h, :].bitcast(F32),
                                ALU.subtract).then_inc(act_ready, 1)

            wait(ca, "mo1")
            for h in heads4:
                wait(mp, f"rms{h}")
                v.tensor_tensor(num[:, h, :], num[:, h, :], ps[:, h % 2, :], ALU.mult) \
                    .then_inc(md.sem, md.one(f"n{h}"))
                wait(md, f"n{h}")
                v.scalar_tensor_tensor(out=num[:, h, :], in0=num[:, h, :], scalar=col("mlnorm", h),
                                       in1=mo[:, h, :], op0=ALU.mult, op1=ALU.mult) \
                    .then_inc(md.sem, md.one(f"m{h}"))
                if h:
                    mlstm_low(h - 1)
            mlstm_low(3)

            for t in range(DT):
                add_squares(t, MEM)
            lo_next(AT["out2"])
            invert(MEM // P)

            def memory_tile(t):
                if t >= 2:
                    dve.wait_ge(mem_ready, t - 1)
                v.scalar_tensor_tensor(out=mem32[t % 2][:], in0=mt[:, t, :],
                                       scalar=col("memn", t), in1=ps[:, 5, 0:MEM], op0=ALU.mult,
                                       op1=ALU.mult).then_inc(normed_ready, 1)
                dve.wait_ge(mem_hi, t + 1)
                v.tensor_tensor(mn_lo[:, t, :], mem32[t % 2][:], mn_hi[:, t, :].bitcast(F32),
                                ALU.subtract).then_inc(mem_ready, 1)

            final_updates(AT["out2"], None, 0, between=memory_tile)

            def memory_block(q):
                b = AT["memk"] + q
                lo_next(b)
                dve.wait_ge(block_done, done(b))
                if q < 4:
                    v.tensor_copy(kx[:, 2 * q:2 * q + 2, :], banks(b)[:, :, 0:MEM]) \
                        .then_inc(block_used, 1)
                else:
                    v.tensor_copy(vx[:, :, 256 * (q - 4):256 * (q - 4) + 256],
                                  ps[:, 2 * (b % 2), :].rearrange("p (i n) -> p i n", n=256)) \
                        .then_inc(block_used, 1)

            memory_block(0)
            invert()
            for q in range(1, 8):
                memory_block(q)
                if q <= 4:
                    for t in (2 * q - 2, 2 * q - 1):
                        post(t, "mixpost")
                    for t in (2 * q - 2, 2 * q - 1):
                        add_squares(t)
                if q == 5:
                    invert()
            prenorm()
            for q in range(4):
                take(AT["xq"] + q, qx[:, 2 * q:2 * q + 2, :], MEM ** -0.5)
            attention(L2, L3)
            final_updates(AT["xo"], None, 0)
            invert()
            for t in range(DT):
                post(t, "xpost")
                if t:
                    add_squares(t - 1)
            add_squares(DT - 1)
            invert()
            prenorm()
            ffn(AT["ffn3"], None)
            invert()
            for t in range(DT):
                post(t, "fpost")


def local_head(i):
    j, a = divmod(i, 2)
    return (j // 4) * 8 + 4 * a + j % 4


def sparse_head(i):
    j, a = divmod(i, 2)
    return 4 * a + j


def heads_to_rows(head_of, n):
    return np.concatenate([np.arange(HD) + HD * head_of(i) for i in range(n)])


def tiles(w):
    rows, n = w.shape
    out = np.zeros((P, DT, n), w.dtype)
    out[:, :rows // P] = w.reshape(rows // P, P, n).transpose(1, 0, 2)
    return out


def weight_blocks(a):
    blocks = []

    def add(*parts):
        blocks.append(np.concatenate([tiles(w) for w in parts], axis=2))

    def pairs(w):
        for j in range(0, w.shape[1], 2 * P):
            add(w[:, j:j + 2 * P])

    def ffn(gu, down):
        first = 0
        for n in THIRDS:
            for j in range(first, first + n):
                add(gu[:, j * P:j * P + P], gu[:, FF + j * P:FF + j * P + P])
            pairs(down[first * P:(first + n) * P])
            first += n

    def cut(w, sizes):
        return np.split(w, np.cumsum(sizes)[:-1], axis=1)

    ffn(a["w1_gu"][0], a["w1_down"][0])
    b_g, c_g, u, q, k, v, zc, za = cut(a["w_in"][0], [D, D, D, D, 256, 256, D, D])
    for i in range(4):
        for j in (2 * i, 2 * i + 1):
            add(c_g[:, j * P:j * P + P], u[:, j * P:j * P + P])
        add(b_g[:, 2 * i * P:2 * i * P + 2 * P])
    rows = heads_to_rows(local_head, 16)
    for j in range(DT):
        add(zc[:, j * P:j * P + P], a["w_conv_proj"][0][:, j * P:j * P + P])
    pairs(q[:, rows])
    pairs(k)
    pairs(v)
    for j in range(DT):
        add(za[:, j * P:j * P + P], a["w_attn_proj"][0][rows][:, j * P:j * P + P])
    pairs(a["w_out"][0])
    ffn(a["w2_gu"][0], a["w2_down"][0])

    nq, kc, vc, ks, vs, kw, vw, gt, mq, mk, mv, mi, mf, mo = cut(
        a["w_in_2"][0], [512] + [128] * 6 + [24, 256, 256, 512, 4, 4, 512])
    misc = np.zeros((D, 2 * P), nq.dtype)
    misc[:, 0:P:32] = mi
    misc[:, 1:25] = gt
    misc[:, P::32] = mf
    add(misc)
    add(kc, vc)
    add(vs, vw)
    add(ks, kw)
    rows = heads_to_rows(sparse_head, 8)
    pairs(nq[:, rows])
    for w in (mq, mk, mv, mo):
        pairs(w)
    for w in (a["cmp_w1_k_2"][0], a["cmp_w1_v_2"][0]):
        add(w[:D])
        add(w[D:])
    w_out = a["w_out_2"][0]
    pairs(np.concatenate([w_out[rows], w_out[512:]]))
    pairs(a["w_xkv_2"][0])
    pairs(a["w_xq_2"][0])
    pairs(a["w_xo_2"][0])
    ffn(a["w_gate_up_2"][0], a["w_down_2"][0])
    assert len(blocks) == NB
    return np.stack(blocks).reshape(-1)


def ada_blocks(w):
    return np.ascontiguousarray(w.reshape(DT // 2, 2, P, 9, D).transpose(3, 0, 2, 1, 4)).reshape(-1)


def columns(a):
    out = np.zeros((P, NCOL), np.float32)

    def put(name, vec):
        part = np.asarray(vec).reshape(-1, P).T
        out[:, CAT[name]:CAT[name] + part.shape[1]] = part

    for name, key in (("c", "c"), ("b_ada", "b_ada"), ("g_ffn1", "g_ffn1"), ("g_mix", "g_mix"),
                      ("g_ffn2", "g_ffn2"), ("g_final", "g_final"), ("conv", "conv_w"),
                      ("mixpre", "mix_norm_pre_2"), ("mixpost", "mix_norm_post_2"),
                      ("xpre", "xattn_norm_pre_2"), ("memn", "mem_norm_2"),
                      ("xpost", "xattn_norm_post_2"), ("fpre", "ffn_norm_pre_2"),
                      ("fpost", "ffn_norm_post_2"), ("conv2", "conv_w_2"), ("conv2b", "conv_b_2"),
                      ("mlnorm", "mlstm_norm_2"), ("pos_k", "cmp_pos_k_2"), ("pos_v", "cmp_pos_v_2")):
        put(name, a[key])
    sinks = a["sinks"][0]
    for i in range(16):
        out[:, CAT["sinks"] + i] = sinks[local_head(i)]
    for i in range(2):
        out[::32, CAT["gate_bias"] + i] = a["mlstm_gate_bias_2"][0, i]
    return out


def constants():
    out = np.zeros((P, NCONST), np.float32)

    def put(name, value):
        out[:, KAT[name]:KAT[name] + value.shape[1]] = value

    p = np.arange(P)
    put("ident", np.eye(P))
    rot = np.zeros((P, P))
    for m in range(P):
        d = m % HD
        src = m + HD // 2 if d < HD // 2 else m - HD // 2
        rot[src, m] = -1.0 if d < HD // 2 else 1.0
    put("rot", rot)
    put("swap", np.eye(P)[(p + 64) % P])
    put("tri", (np.arange(S)[None, :] >= p[:, None]).astype(np.float32))
    freq = (1.0 / np.float32(10000.0) ** (np.arange(0, HD, 2, dtype=np.float32) / np.float32(HD)))
    ang = freq.astype(np.float32)[p % (HD // 2)][:, None] * np.arange(S, dtype=np.float32)[None, :]
    put("cos", np.cos(ang))
    put("sin", np.sin(ang))
    diff = P + p[:, None] - np.arange(2 * P)[None, :]
    put("mask", np.where((diff >= 0) & (diff < P), 0.0, NEG))
    put("maskT", np.where(p[None, :] >= p[:, None], 0.0, NEG))
    put("valid", (p[:, None] >= 31).astype(np.float32))
    return out


def bias_selector():
    buckets, far = 32, 128
    dist = S - 1 - np.arange(NDIST)
    n = np.maximum(dist, 0)
    half = buckets // 2
    nf = np.maximum(n, 1).astype(np.float32)
    large = half + (np.log(nf / half) / np.float32(np.log(far / half)) * half).astype(np.int32)
    bucket = np.where(n < half, n, np.minimum(large, buckets - 1))
    out = np.zeros((33, NDIST), np.float32)
    out[bucket, np.arange(NDIST)] = (dist >= 0)
    out[32] = np.where(dist >= 0, 0.0, NEG)
    return out


def kernel(**inputs):
    from concourse import bacc
    from concourse.bass_utils import run_bass_kernel_spmd

    a = {name: np.asarray(value) for name, value in inputs.items()}
    arrays = {
        "x": np.ascontiguousarray(a["x"][0].T.reshape(DT, P, S).transpose(1, 0, 2)),
        "mem": np.ascontiguousarray(a["mem_2"][0].T.reshape(DT, P, MEM).transpose(1, 0, 2)),
        "ada": ada_blocks(a["w_ada"][0]),
        "weights": weight_blocks(a),
        "cols": columns(a),
        "consts": constants(),
        "selector": bias_selector(),
        "rel": np.ascontiguousarray(a["rel_bias_2"].T),
        "w2k": np.ascontiguousarray(a["cmp_w2_k_2"][0]),
        "w2v": np.ascontiguousarray(a["cmp_w2_v_2"][0]),
    }
    nc = bacc.Bacc("TRN2", target_bir_lowering=False, num_devices=1)
    ten = {name: nc.dram_tensor(f"in_{name}", value.shape, F32, kind="ExternalInput").ap()
           for name, value in arrays.items()}
    ten["out"] = nc.dram_tensor("result", (P, DT, S), F32, kind="ExternalOutput").ap()
    build(nc, ten)
    result = run_bass_kernel_spmd(nc, [{f"in_{name}": value for name, value in arrays.items()}],
                                  core_ids=[0]).results[0]["result"]
    return np.ascontiguousarray(result.transpose(1, 0, 2).reshape(D, S).T)[None]
```

```python
from contextlib import ExitStack

import numpy as np

import concourse.bass as bass
from concourse import mybir

F32 = mybir.dt.float32
F32R = mybir.dt.float32r
ALU = mybir.AluOpType
ACT = mybir.ActivationFunctionType
AX = mybir.AxisListType.X

P = 128
S = 512
D = 1024
DT = D // P
NT = S // P
FF = 2816
FT = FF // P
MEM = 256
HD = 64
NEG = -1e30
EPS = 1e-6
THIRDS = (8, 8, 6)
BLOCK = P * DT * 2 * P

SECTIONS = (("ffn1", 34), ("conv", 12), ("zconv", 8), ("q", 4), ("k", 1), ("v", 1), ("za", 4),
            ("attnproj", 4), ("out1", 4), ("ffn2", 34), ("misc", 1), ("kvc", 1), ("vv", 1), ("kk", 1), ("nq", 2),
            ("mq", 1), ("mk", 1), ("mv", 2), ("mo", 2), ("cmp", 4), ("out2", 4), ("memk", 4),
            ("memv", 4), ("xq", 4), ("xo", 4), ("ffn3", 34))
AT, NB = {}, 0
for _name, _n in SECTIONS:
    AT[_name] = NB
    NB += _n
ADA_BLOCKS = 9 * DT // 2
ADA_FIRST = 8
START = 2


def done(b):
    return b + START + 1


def used(b):
    return b + START + 1 - (4 if not isinstance(b, int) or b >= AT["cmp"] + 4 else
                            max(0, b - AT["cmp"] + 1))


COLS = (("c", 8), ("b_ada", 72), ("g_ffn1", 8), ("g_mix", 8), ("g_ffn2", 8), ("g_final", 8),
        ("conv", 24), ("mixpre", 8), ("mixpost", 8), ("xpre", 8), ("memn", 8), ("xpost", 8),
        ("fpre", 8), ("fpost", 8), ("conv2", 16), ("conv2b", 4), ("mlnorm", 4), ("pos_k", 16),
        ("pos_v", 16), ("sinks", 16), ("gate_bias", 2))
CAT, NCOL = {}, 0
for _name, _n in COLS:
    CAT[_name] = NCOL
    NCOL += _n
CONSTS = (("ident", 128), ("rot", 128), ("swap", 128), ("tri", 512), ("cos", 512), ("sin", 512),
          ("mask", 256), ("maskT", 128), ("valid", 1))
KAT, NCONST = {}, 0
for _name, _n in CONSTS:
    KAT[_name] = NCONST
    NCONST += _n
NDIST = S + P


class Steps:

    def __init__(self, sem, names):
        self.sem, self.names, self.given = sem, names, 0
        assert len(set(names)) == len(names)

    def one(self, name):
        assert self.names[self.given] == name, (name, self.names[self.given])
        self.given += 1
        return 1

    def at(self, name):
        return self.names.index(name) + 1


def build(nc, ten):
    ctx = ExitStack()
    with ctx:
        def sem(name):
            return ctx.enter_context(nc.semaphore(name))

        def alloc(stack, name, shape, dt=F32):
            return stack.enter_context(nc.sbuf_tensor(name, shape, dt))

        def sb(name, shape, dt=F32):
            return alloc(ctx, name, shape, dt)

        x = sb("x", [P, DT, S])
        act_hi, act_lo = sb("act_hi", [P, DT, S], F32R), sb("act_lo", [P, DT, S], F32R)
        raw = [sb(f"raw{k}", [P, DT, 256]) for k in range(2)]
        w_hi = [sb(f"w_hi{k}", [P, DT, 256], F32R) for k in range(2)]
        w_lo = [sb(f"w_lo{k}", [P, DT, 256], F32R) for k in range(2)]
        cols = sb("cols", [P, NCOL])
        consts = sb("consts", [P, NCONST])
        mods = sb("mods", [P, 72])
        gains = sb("gains", [P, 5, DT])
        negsink = sb("negsink", [P, 16])
        zeros = sb("zeros", [P, 256])
        c_act = sb("c_act", [P, DT])
        ones = sb("ones", [P, P])
        eps = sb("eps", [P, 1])
        normed = [sb(f"normed{k}", [P, S]) for k in range(2)]
        act32 = [sb(f"act32_{k}", [P, S]) for k in range(2)]
        square = [sb(f"square{k}", [P, S]) for k in range(2)]
        sumsq = sb("sumsq", [P, S])
        root, rinv = sb("root", [P, NT]), sb("rinv", [P, NT])
        w2 = sb("w2", [P, 2, 2, HD])
        ps = ctx.enter_context(nc.psum_tensor("ps", [P, 8, S], F32))

        smax = [sb(f"smax{k}", [P, 2]) for k in range(3)]
        nmx = [sb(f"nmx{k}", [P, 2]) for k in range(3)]
        den = [sb(f"den{k}", [P, 2]) for k in range(3)]
        sinkd = [sb(f"sinkd{k}", [P, 2]) for k in range(3)]
        sinke = [sb(f"sinke{k}", [P, 2]) for k in range(3)]
        inv = [sb(f"inv{k}", [P, 2]) for k in range(3)]

        with ExitStack() as s:
            selector = alloc(s, "selector", [33, NDIST])
            rel = alloc(s, "rel", [33, 8])
            relb = alloc(s, "relb", [33, 8, P])
            biasrow = [alloc(s, f"biasrow{k}", [P, NDIST]) for k in range(2)]
        with ExitStack() as s:
            hid_hi, hid_lo = alloc(s, "hid_hi", [P, 8, S], F32R), alloc(s, "hid_lo", [P, 8, S], F32R)
            y = alloc(s, "y", [P, DT, S])
            with ExitStack() as t:
                silu = [alloc(t, f"silu{k}", [P, S]) for k in range(2)]
                prod = [alloc(t, f"prod{k}", [P, S]) for k in range(2)]
                ada_raw = [alloc(t, f"ada_raw{k}", [P, 2, D]) for k in range(2)]
                ada_acc = [alloc(t, f"ada_acc{k}", [P, D]) for k in range(2)]
            with ExitStack() as t:
                cgate = [alloc(t, f"cgate{k}", [P, S]) for k in range(2)]
                cu = [alloc(t, f"cu{k}", [P, S + 2]) for k in range(2)]
                conv = [alloc(t, f"conv{k}", [P, S]) for k in range(2)]
                bconv = [alloc(t, f"bconv{k}", [P, S]) for k in range(2)]
            with ExitStack() as t:
                q1 = alloc(t, "q1", [P, 8, S])
                k1 = alloc(t, "k1", [P, 2, S])
                v1 = alloc(t, "v1", [P, NT, 256])
                with ExitStack() as r:
                    sig = [alloc(r, f"sig{k}", [P, S]) for k in range(2)]
                with ExitStack() as r:
                    unrot = [alloc(r, f"unrot{k}", [P, 2, S]) for k in range(2)]
                    rcos = alloc(r, "rcos", [P, 2, S])
                with ExitStack() as r:
                    sc1 = [alloc(r, f"sc1_{k}", [P, 2, 256]) for k in range(3)]
                    pt1 = [alloc(r, f"pt1_{k}", [P, 2, 256]) for k in range(2)]
        with ExitStack() as s:
            kk = alloc(s, "kk", [P, 2, S])
            vv = alloc(s, "vv", [P, NT, 256])
            nq = alloc(s, "nq", [P, 4, S])
            mqk = alloc(s, "mqk", [P, 4, S])
            mv = alloc(s, "mv", [P, NT, S])
            mo = alloc(s, "mo", [P, 4, S])
            irow, frow = alloc(s, "irow", [P, S]), alloc(s, "frow", [P, S])
            gT = alloc(s, "gT", [P, NT, P])
            kcmp, vcmp = alloc(s, "kcmp", [P, 32]), alloc(s, "vcmp", [32, P])
            with ExitStack() as t:
                kvc, kvs = alloc(t, "kvc", [P, 2, S]), alloc(t, "kvs", [P, 2, S])
                cb = alloc(t, "cb", [P, 16, 62])
                cb_hi = [alloc(t, f"cb_hi{i}", [P, 16, 62], F32R) for i in range(2)]
                cb_lo = [alloc(t, f"cb_lo{i}", [P, 16, 62], F32R) for i in range(2)]
                gsig = alloc(t, "gsig", [P, S])
                with ExitStack() as r:
                    upad = alloc(r, "upad", [P, 2, S + 3])
                    usum = alloc(r, "usum", [P, 2, S])
                with ExitStack() as r:
                    hc = alloc(r, "hc", [64, 2, 256])
                    hcT = alloc(r, "hcT", [P, 2, 2, 62])
            with ExitStack() as t:
                table = alloc(t, "table", [P, 8, S])
                sc2 = [alloc(t, f"sc2_{k}", [P, 2, S]) for k in range(3)]
                pt2 = [alloc(t, f"pt2_{k}", [P, 2, S]) for k in range(2)]
            with ExitStack() as t:
                lfT = alloc(t, "lfT", [P, NT, P])
                aT = alloc(t, "aT", [P, NT, P])
                run = [alloc(t, f"run{k}", [P, S]) for k in range(2)]
                arow = alloc(t, "arow", [P, S])
                emrow = alloc(t, "emrow", [P, S])
                nmax = [alloc(t, f"nmax{k}", [P, S]) for k in range(2)]
                wt = [alloc(t, f"wt{k}", [P, S]) for k in range(2)]
                diag = [alloc(t, f"diag{k}", [P, P]) for k in range(2)]
                drow, dinv = alloc(t, "drow", [P, S]), alloc(t, "dinv", [P, S])
                num = alloc(t, "num", [P, 4, S])
                square4 = [*wt, *nmax]
        with ExitStack() as s:
            alloc(s, "hid_hi_hole", [P, 8, S]), alloc(s, "hid_lo_hole", [P, 8, S])
            alloc(s, "y_hole", [P, DT, S])
            kx = alloc(s, "kx", [P, DT, MEM])
        with ExitStack() as s:
            mn_hi, mn_lo = alloc(s, "mn_hi", [P, DT, MEM], F32R), alloc(s, "mn_lo", [P, DT, MEM], F32R)
            qx = alloc(s, "qx", [P, DT, S])
            alloc(s, "y_hole2", [P, DT, S])
            alloc(s, "kx_hole", [P, DT, MEM])
            vx = alloc(s, "vx", [P, 2, D])
            mt = alloc(s, "mt", [P, DT, MEM])
            mem32 = [alloc(s, f"mem32_{k}", [P, MEM]) for k in range(2)]
            with ExitStack() as t:
                sc3 = [alloc(t, f"sc3_{k}", [P, 2, 256]) for k in range(3)]
                pt3 = [alloc(t, f"pt3_{k}", [P, 2, 256]) for k in range(2)]
        scratch = nc.dram_tensor("bias_rows", (8, P, NDIST), F32, kind="Internal").ap()

        def col(name, i=0, n=1):
            return cols[:, CAT[name] + i:CAT[name] + i + n]

        def const(name, n=None):
            width = dict(CONSTS)[name] if n is None else n
            return consts[:, KAT[name]:KAT[name] + width]

        ident = const("ident")

        x_in, cols_in, consts_in, w2_in = sem("x_in"), sem("cols_in"), sem("consts_in"), sem("w2_in")
        sel_in, rel_in, mem_in = sem("sel_in"), sem("rel_in"), sem("mem_in")
        raw_in = [sem("raw_in0"), sem("raw_in1")]
        split_hi, split_lo = sem("split_hi"), sem("split_lo")
        block_done, block_used = sem("block_done"), sem("block_used")
        half_done, half_used = sem("half_done"), sem("half_used")
        ada_in = [sem("ada_in0"), sem("ada_in1")]
        ada_step, ada_sum = sem("ada_step"), sem("ada_sum")
        ada_zero = sem("ada_zero")
        filled, v_step = sem("filled"), sem("v_step")
        c_ready, mods_ready = sem("c_ready"), sem("mods_ready")
        sq_ready, sumsq_step = sem("sq_ready"), sem("sumsq_step")
        ms_ready, root_ready = sem("ms_ready"), sem("root_ready")
        rinv_ready, rstd_ready = sem("rinv_ready"), sem("rstd_ready")
        normed_ready, act32_ready, act_ready = sem("normed_ready"), sem("act32_ready"), sem("act_ready")
        x_ready, mem_hi, mem_ready = sem("x_ready"), sem("mem_hi"), sem("mem_ready")
        silu_ready, hid_ready = sem("silu_ready"), sem("hid_ready")
        relb_ready, brow_sum, brow_copied = sem("relb_ready"), sem("brow_sum"), sem("brow_copied")
        brow_out = [sem("brow_out0"), sem("brow_out1")]
        table_in = sem("table_in")
        cgate_ready, sig_ready, merged_ready = sem("cgate_ready"), sem("sig_ready"), sem("merged_ready")
        merged_hi = sem("merged_hi")
        unrot_ready, rot_sum, rope_done = sem("unrot_ready"), sem("rot_sum"), sem("rope_done")
        scores_ready, biased, negmax_ready = sem("scores_ready"), sem("biased"), sem("negmax_ready")
        exp_done, probs_ready, turned = sem("exp_done"), sem("probs_ready"), sem("turned")
        turned_a, turned_b, pv_done = sem("turned_a"), sem("turned_b"), sem("pv_done")
        out_hi, out_lo = sem("out_hi"), sem("out_lo")
        y_out = sem("y_out")

        heads4 = range(4)
        cp = Steps(sem("cmp_pe"), ["gateT", "swap", "hiddenT", "kcmp", "vcmp"])
        ca = Steps(sem("cmp_act"), ["gsig", "gT", "kvs", "hi0", "hi1", "mq", "mk", "mo0", "mo1",
                                    "hidden0", "hidden1", "hiddenT"])
        cd = Steps(sem("cmp_dve"), ["cb0", "lo0", "cb1", "lo1", "conv0", "conv1", "mk", "kcmp",
                                    "vcmp"])
        mp = Steps(sem("mlstm_pe"), ["lfT", "F", "aT"] + [
            s for h in heads4 for s in [f"max{h}", f"scores{h}0"] + [
                r for kb in range(1, 4) for r in (f"scores{h}{kb}", f"value{h}{kb - 1}")]
            + [f"value{h}3"]] + [f"dinv{h}" for h in heads4] + [f"sum{h}" for h in heads4]
            + [f"rms{h}" for h in heads4])
        ma = Steps(sem("mlstm_act"), ["exp", "ln", "lfT", "aT", "em"] + [
            s for h in heads4 for s in [f"nmax{h}"] + [f"w{h}{kb}" for kb in heads4] + [f"num{h}"]]
            + ["den"] + [f"square{h}" for h in heads4] + ["root"] + [f"hi{h}" for h in heads4])
        md = Steps(sem("mlstm_dve"), ["nabs", "lf", "a", "pos"] + [f"run{i}{e}" for i in range(9)
                                                                for e in "ab"] + ["nem"] + [
            s for h in heads4 for kb in heads4 for s in (f"diag{h}{kb}", f"s{h}{kb}")]
            + ["nden", "floor", "dinv"] + [f"h{h}" for h in heads4] + ["rinv"]
            + [s for h in heads4 for s in (f"n{h}", f"m{h}")])

        items = [("local", j, n, 0) for j in range(8) for n in range(NT)]
        L1 = len(items)
        items += [("sparse", j, n, br) for j in range(4) for n in range(NT) for br in range(3)]
        L2 = len(items)
        items += [("cross", h, pair, 0) for h in range(4) for pair in range(2)]
        L3 = len(items)

        def nkeys(g):
            ph, j, n, br = items[g]
            if ph == "local":
                return 128 if n == 0 else 256
            if ph == "sparse":
                return 8 * n + 7 if br == 0 else 128 * (n + 1)
            return MEM

        def sc(g):
            return {"local": sc1, "sparse": sc2, "cross": sc3}[items[g][0]][g % 3]

        def pt(g):
            return {"local": pt1, "sparse": pt2, "cross": pt3}[items[g][0]][g % 2]

        def key_tiles(g):
            n = nkeys(g)
            return [(k, min(128, n - k)) for k in range(0, n, 128)]

        def out_tiles(g):
            ph, j, n, br = items[g]
            if ph == "local":
                return [(j, 6)] if n == NT - 1 else []
            if ph == "sparse":
                return [(j, 6)] if (n, br) == (NT - 1, 2) else []
            return [(2 * j, 6), (2 * j + 1, 7)] if n == 1 else []

        outs_before = [sum(len(out_tiles(i)) for i in range(g)) for g in range(L3 + 1)]

        def fill_half(r):
            return r // 8, (r // 4) % 2, r % 4

        def hid_base(ffn, third):
            return ffn * FT + 8 * third + (8 if ffn else 0)

        def scores_of(g):
            return 2 * (g % 2)

        def gu_loops(n, ada):
            return [(0, 2), (2, n // 2)] if ada else [(0, n // 2)]

        block = ctx.enter_context(nc.Block())

        @block.sync
        def _(sp):
            def load(p, k):
                src = ten["weights"][bass.ds((2 * p + k) * BLOCK, BLOCK)]
                sp.dma_start(raw[k][:].rearrange("p t n -> p (t n)"),
                             src.rearrange("(p n) -> p n", p=P)).then_inc(raw_in[k], 16)

            def next_load(p, k):
                sp.wait_ge(split_lo, 2 * p + k - 1)
                load(p, k)

            def load_ada(b, k):
                src = ten["ada"][bass.ds(b * BLOCK, BLOCK)]
                sp.dma_start(ada_raw[k][:].rearrange("p t n -> p (t n)"),
                             src.rearrange("(p n) -> p n", p=P)).then_inc(ada_in[k], 16)

            def next_ada(b, k):
                sp.wait_ge(ada_step, 2 * b - 2)
                load_ada(b, k)

            load_ada(0, 0)
            load_ada(1, 1)
            sp.dma_start(x[:], ten["x"]).then_inc(x_in, 16)
            for b in range(2, ADA_FIRST):
                next_ada(b, b % 2)
            load(0, 0)
            load(0, 1)
            next_ada(ADA_FIRST, 0)
            late = (ADA_BLOCKS - ADA_FIRST) // 2
            with sp.Fori(1, late) as p:
                for k in range(2):
                    next_load(p, k)
                    next_ada(2 * p + k + ADA_FIRST - 1, 1 - k)
            next_load(late, 0)
            next_ada(ADA_BLOCKS - 1, 1)
            next_load(late, 1)
            with sp.Fori(late + 1, NB // 2) as p:
                for k in range(2):
                    next_load(p, k)
            for t in range(DT):
                sp.wait_ge(x_ready, 3 * DT + t + 1)
                sp.dma_start(ten["out"][:, t, :], x[:, t, :]).then_inc(y_out, 16)
            sp.wait_ge(y_out, 16 * DT)

        @block.tensor
        def _(pe):
            norms = [0]

            def mm(out, lhsT, rhs, start=True, stop=True):
                return nc.tensor.matmul(out, lhsT, rhs, start=start, stop=stop)

            def wait(steps, name):
                pe.wait_ge(steps.sem, steps.at(name))

            def block_fm(p, k, sources, ready=None, tiles=DT, n=S, offset=0):
                b = 2 * p + k
                pe.wait_ge(split_lo, b + 1)
                pe.wait_ge(block_used, b + 1 - offset)
                for t in range(tiles):
                    if ready is not None:
                        pe.wait_ge(ready[0], ready[1] + t + 1)
                    for u in range(2):
                        hi, lo = sources[u]
                        cut = slice(u * P, u * P + P)
                        out = ps[:, 2 * k + u, 0:n]
                        mm(out, w_hi[k][:, t, cut], hi[:, t, 0:n], t == 0, False)
                        mm(out, w_hi[k][:, t, cut], lo[:, t, 0:n], False, False)
                        last = mm(out, w_lo[k][:, t, cut], hi[:, t, 0:n], False, t == tiles - 1)
                last.then_inc(block_done, 1)

            def block_tm(p, k, hi, lo, tokens=NT, offset=0):
                b = 2 * p + k
                pe.wait_ge(split_lo, b + 1)
                pe.wait_ge(block_used, b + 1 - offset)
                for i in range(tokens):
                    out = ps[:, 2 * k + i // 2, (i % 2) * 256:(i % 2) * 256 + 256]
                    cut = slice(i * P, i * P + P)
                    for t in range(DT):
                        mm(out, hi[:, t, cut], w_hi[k][:, t, :], t == 0, False)
                        mm(out, lo[:, t, cut], w_hi[k][:, t, :], False, False)
                        last = mm(out, hi[:, t, cut], w_lo[k][:, t, :], False, t == DT - 1)
                last.then_inc(block_done, 1)

            def stats(blocks=NT):
                nn = norms[0]
                pe.wait_ge(sumsq_step, 7 * (nn + 1))
                for i in range(blocks):
                    last = mm(ps[:, 4, i:i + 1], sumsq[:, i * P:i * P + P], ones[:, 0:1])
                last.then_inc(ms_ready, 1)
                pe.wait_ge(rinv_ready, nn + 1)
                for i in range(blocks):
                    last = mm(ps[:, 5, i * P:i * P + P], rinv[:, i:i + 1].to_broadcast([P, P]), ident)
                last.then_inc(rstd_ready, 1)
                norms[0] += 1

            def ada_columns(g):
                pe.wait_ge(ada_step, DT * (g + 1))
                for j in range(DT):
                    last = mm(ps[:, 7, g * DT + j:g * DT + j + 1], ada_acc[g % 2][:, j * P:j * P + P],
                              ones[:, 0:1])
                last.then_inc(ada_sum, 1)

            def ffn(idx, b0, act_base, offset=0):
                src = [(act_hi, act_lo)] * 2
                hid = [(hid_hi, hid_lo)] * 2
                ada = idx == 0
                groups = iter([None, *range(2, 9)] if ada else [])
                for third, n in enumerate(THIRDS):
                    s = (b0 + 12 * third) // 2
                    for first, end in gu_loops(n, ada):
                        with pe.Fori(first, end) as i:
                            for k in range(2):
                                block_fm(s + i, k, src, (act_ready, act_base), offset=offset)
                        g = next(groups, None)
                        if g is not None:
                            ada_columns(g)
                    s += n // 2
                    with pe.Fori(0, 2) as i:
                        for k in range(2):
                            block_fm(s + i, k, hid, (hid_ready, hid_base(idx, third)), tiles=n,
                                     offset=offset)
                    g = next(groups, None)
                    if g is not None:
                        ada_columns(g)

            def attention(g0, g1, fill=None, halves=0):
                def part(r):
                    m, u, c = fill_half(r)
                    b = fill + m
                    k = b % 2
                    if c == 0 and u == 0:
                        pe.wait_ge(split_lo, b + 1)
                        if m:
                            pe.wait_ge(block_used, used(b - 1))
                    if c == 0 and u == 1:
                        pe.wait_ge(half_used, halves + m + 1)
                    cut = slice(u * P, u * P + P)
                    for t in (2 * c, 2 * c + 1):
                        out = ps[:, 7, :]
                        mm(out, w_hi[k][:, t, cut], act_hi[:, t, :], t == 0, False)
                        mm(out, w_hi[k][:, t, cut], act_lo[:, t, :], False, False)
                        last = mm(out, w_lo[k][:, t, cut], act_hi[:, t, :], False, t == DT - 1)
                    if c == 3:
                        last.then_inc(block_done if u else half_done, 1)

                def scores(g):
                    ph, j, n, br = items[g]
                    if g - g0 >= 2:
                        pe.wait_ge(biased, g - 1)
                    nk = nkeys(g)
                    for a in range(2):
                        out = ps[:, scores_of(g) + a, 0:nk]
                        half = slice(64 * a, 64 * a + 64)
                        if ph == "local":
                            k0 = P * (n - 1) if n else 0
                            last = mm(out, q1[half, j, n * P:n * P + P], k1[half, j // 4, k0:k0 + nk])
                        elif ph == "sparse":
                            key = kcmp[half, 0:nk] if br == 0 else kk[half, br - 1, 0:nk]
                            last = mm(out, nq[half, j, n * P:n * P + P], key)
                        else:
                            i = 2 * n + a
                            for e in range(2):
                                last = mm(out, qx[:, 2 * j + e, i * P:i * P + P],
                                          kx[:, 2 * j + e, :], e == 0, e == 1)
                    last.then_inc(scores_ready, 1)

                def turn(g):
                    pe.wait_ge(probs_ready, g + 1)
                    if g > g0:
                        pe.wait_ge(turned_a, g)
                        pe.wait_ge(turned_b, g)
                    for a in range(2):
                        for k, w in key_tiles(g):
                            last = nc.tensor.transpose(ps[0:w, 4 + a, k:k + P], sc(g)[:, a, k:k + w],
                                                       ident)
                    last.then_inc(turned, 1)

                def product(g):
                    ph, j, n, br = items[g]
                    pe.wait_ge(turned_a, g + 1)
                    pe.wait_ge(turned_b, g + 1)
                    if ph == "cross":
                        if n == 0 and j:
                            pe.wait_ge(out_lo, outs_before[g])
                        for a in range(2):
                            m = (2 * n + a) * P
                            for e in range(2):
                                for i in range(2):
                                    f = j * 256 + e * P
                                    last = mm(ps[:, 6 + e, m:m + P], vx[:, i, f:f + P],
                                              pt(g)[:, a, i * P:i * P + P], i == 0, i == 1)
                        last.then_inc(pv_done, 1)
                        return
                    if n == 0 and br == 0 and j:
                        pe.wait_ge(out_lo, outs_before[g])
                    tiles = key_tiles(g)
                    for a in range(2):
                        out = ps[64 * a:64 * a + 64, 6, n * P:n * P + P]
                        for i, (k, w) in enumerate(tiles):
                            if ph == "local":
                                f = (j // 4) * P + 64 * a
                                v = v1[:, (n - 1 if n else 0) + i, f:f + 64]
                                start, stop = i == 0, i == len(tiles) - 1
                            elif br == 0:
                                v = vcmp[0:w, 64 * a:64 * a + 64]
                                start, stop = True, False
                            else:
                                f = (br - 1) * P + 64 * a
                                v = vv[:, i, f:f + 64]
                                start, stop = False, br == 2 and i == len(tiles) - 1
                            last = mm(out, v, pt(g)[0:w, a, k:k + P], start, stop)
                    last.then_inc(pv_done, 1)

                for g in range(g0, g0 + 3):
                    scores(g)
                for g in range(g0, g1):
                    if g + 3 < g1:
                        scores(g + 3)
                    if fill is not None:
                        part(g - g0)
                    if g > g0:
                        product(g - 1)
                    turn(g)
                product(g1 - 1)

            pe.wait_ge(sel_in, 16)
            pe.wait_ge(relb_ready, 1)
            for h in range(8):
                if h:
                    pe.wait_ge(brow_copied, h)
                mm(ps[:, 2, :], relb[:, h, :], selector[:, 0:S])
                mm(ps[:, 3, 0:NDIST - S], relb[:, h, :], selector[:, S:NDIST]).then_inc(brow_sum, 1)
            for k in range(START):
                mm(ps[:, 6, k:k + 1], ones[:], ones[:, 0:1]).then_inc(block_done, 1)
            pe.wait_ge(consts_in, 16)
            for g in range(2):
                ada_columns(g)
            stats()
            ffn(0, AT["ffn1"], 0)

            act = [(act_hi, act_lo)] * 2
            stats()
            with pe.Fori(0, 6) as i:
                for k in range(2):
                    block_fm(AT["conv"] // 2 + i, k, act, (act_ready, 8))
            mix = [(act_hi, act_lo), (hid_hi, hid_lo)]
            with pe.Fori(0, 4) as i:
                for k in range(2):
                    block_fm(AT["zconv"] // 2 + i, k, mix, (hid_ready, FT))

            def rotate(r, k):
                pe.wait_ge(unrot_ready, r + 1)
                if r:
                    pe.wait_ge(rope_done, r)
                for u in range(2):
                    last = mm(ps[:, 4 + u, :], const("rot"), unrot[k][:, u, :])
                last.then_inc(rot_sum, 1)

            for r in range(5):
                b = AT["q"] + r
                block_fm(b // 2, b % 2, act)
                if r:
                    rotate(r - 1, (b - 1) % 2)
            block_tm(AT["v"] // 2, 1, act_hi, act_lo)
            rotate(4, 0)
            pe.wait_ge(block_used, used(AT["v"]))
            pe.wait_ge(rope_done, 5)
            attention(0, L1, AT["za"])
            pe.wait_ge(out_lo, outs_before[L1])
            with pe.Fori(0, 2) as i:
                for k in range(2):
                    block_fm(AT["attnproj"] // 2 + i, k, [(hid_hi, hid_lo)] * 2)
            with pe.Fori(0, 2) as i:
                for k in range(2):
                    block_fm(AT["out1"] // 2 + i, k, act, (act_ready, 16))
            stats()
            ffn(1, AT["ffn2"], 24)

            stats()
            stats()
            block_fm(AT["misc"] // 2, 0, act, (act_ready, 32))
            block_fm(AT["kvc"] // 2, 1, act)
            block_tm(AT["vv"] // 2, 0, act_hi, act_lo)
            wait(ca, "gsig")
            for i in range(NT):
                last = nc.tensor.transpose(ps[:, 6, i * P:i * P + P], gsig[:, i * P:i * P + P], ident)
            last.then_inc(cp.sem, cp.one("gateT"))
            pe.wait_ge(block_used, used(AT["kvc"]))
            for u in range(2):
                last = mm(ps[:, 4 + u, :], const("swap"), kvc[:, u, :])
            last.then_inc(cp.sem, cp.one("swap"))
            block_fm(AT["kk"] // 2, 1, act)
            for b in range(AT["nq"], AT["mv"]):
                block_fm(b // 2, b % 2, act)
            for b in range(AT["mv"], AT["mo"]):
                block_tm(b // 2, b % 2, act_hi, act_lo)
            for b in range(AT["mo"], AT["cmp"]):
                block_fm(b // 2, b % 2, act)
            wait(ca, "kvs")
            for e in range(2):
                wait(cd, f"lo{e}")
                for half in range(2):
                    b = AT["cmp"] + 2 * e + half
                    pe.wait_ge(split_lo, b + 1)
                    for t in range(DT):
                        j, k = 8 * half + t, b % 2
                        out = ps[0:62, 4 + e, 0:256]
                        mm(out, cb_hi[e][:, j, :], w_hi[k][:, t, :], j == 0, False)
                        mm(out, cb_lo[e][:, j, :], w_hi[k][:, t, :], False, False)
                        last = mm(out, cb_hi[e][:, j, :], w_lo[k][:, t, :], False, j == 15)
                    last.then_inc(block_done, 1)
            wait(ca, "hidden1")
            wait(ca, "gT")
            for e in range(2):
                for i in range(2):
                    last = nc.tensor.transpose(ps[:, 6, (2 * e + i) * 64:(2 * e + i) * 64 + 62],
                                               hc[0:62, e, i * P:i * P + P], ident[0:62, 0:62])
            last.then_inc(cp.sem, cp.one("hiddenT"))
            wait(ca, "hiddenT")
            pe.wait_ge(w2_in, 32)
            for a in range(2):
                for i in range(2):
                    last = mm(ps[64 * a:64 * a + 64, 7, 0:31], w2[:, 0, i, :],
                              hcT[:, 0, i, 31 * a:31 * a + 31], i == 0, i == 1)
            last.then_inc(cp.sem, cp.one("kcmp"))
            for a in range(2):
                for i in range(2):
                    last = mm(ps[0:31, 4, 64 * a:64 * a + 64], hcT[:, 1, i, 31 * a:31 * a + 31],
                              w2[:, 1, i, :], i == 0, i == 1)
            last.then_inc(cp.sem, cp.one("vcmp"))
            wait(cd, "vcmp")
            pe.wait_ge(block_used, used(AT["mo"] + 1))
            attention(L1, L2)

            pe.wait_ge(out_lo, outs_before[L2])
            wait(md, "lf")
            for i in range(NT):
                last = nc.tensor.transpose(ps[:, 0, i * P:i * P + P], frow[:, i * P:i * P + P], ident)
            last.then_inc(mp.sem, mp.one("lfT"))
            wait(ma, "lfT")
            for i in range(NT):
                last = mm(ps[:, 1, i * P:S], lfT[:, i, :], const("tri", S - i * P), i == 0, i == NT - 1)
            last.then_inc(mp.sem, mp.one("F"))
            wait(md, "a")
            for i in range(NT):
                last = nc.tensor.transpose(ps[:, 0, i * P:i * P + P], arow[:, i * P:i * P + P], ident)
            last.then_inc(mp.sem, mp.one("aT"))
            wait(md, "run8b")

            def value(h, kb):
                wait(md, f"s{h}{kb}")
                if kb == 0 and h:
                    wait(ma, f"num{h - 1}")
                part = wt[(4 * h + kb) % 2][:, kb * P:S]
                mm(ps[:, 6, kb * P:S], mv[:, kb, h * P:h * P + P], part, kb == 0, kb == 3)
                mm(ps[32 * h:32 * h + 32, 7, kb * P:S], ones[:, 0:32], part, kb == 0, kb == 3) \
                    .then_inc(mp.sem, mp.one(f"value{h}{kb}"))

            for h in heads4:
                row = slice(32 * h, 32 * h + 1)
                half = slice(64 * (h % 2), 64 * (h % 2) + 64)
                if h:
                    wait(ma, f"nmax{h - 1}")
                mm(ps[:, 2, :], ones[row, :], run[1][row, :]).then_inc(mp.sem, mp.one(f"max{h}"))
                for kb in range(NT):
                    c = 4 * h + kb
                    if c >= 2:
                        wait(md, f"s{(c - 2) // 4}{(c - 2) % 4}")
                    mm(ps[:, 4 + c % 2, 0:S - kb * P], mqk[half, 2 + h // 2, kb * P:kb * P + P],
                       mqk[half, h // 2, kb * P:S]).then_inc(mp.sem, mp.one(f"scores{h}{kb}"))
                    if kb:
                        value(h, kb - 1)
                value(h, NT - 1)
            wait(md, "dinv")
            for h in heads4:
                row = slice(32 * h, 32 * h + 1)
                if h >= 2:
                    wait(md, f"h{h - 2}")
                mm(ps[:, h % 2, :], ones[row, :], dinv[row, :]).then_inc(mp.sem, mp.one(f"dinv{h}"))
            for h in heads4:
                wait(ma, f"square{h}")
                mm(ps[32 * h:32 * h + 32, 3, :], ones[:, 0:32], square4[h][:]) \
                    .then_inc(mp.sem, mp.one(f"sum{h}"))
            wait(md, "rinv")
            for h in heads4:
                row = slice(32 * h, 32 * h + 1)
                if h >= 2:
                    wait(md, f"n{h - 2}")
                mm(ps[:, h % 2, :], ones[row, :], dinv[row, :]).then_inc(mp.sem, mp.one(f"rms{h}"))
            wait(md, "m3")

            b = AT["out2"]
            block_fm(b // 2, 0, act, (act_ready, 36), offset=4)
            stats(MEM // P)
            block_fm(b // 2, 1, act, offset=4)
            block_fm(b // 2 + 1, 0, act, offset=4)
            block_fm(b // 2 + 1, 1, act, offset=4)
            memory = [(mn_hi, mn_lo)] * 2
            for q in range(8):
                b = AT["memk"] + q
                if q < 4:
                    block_fm(b // 2, b % 2, memory, (mem_ready, 0), n=MEM, offset=4)
                else:
                    block_tm(b // 2, b % 2, mn_hi, mn_lo, tokens=2, offset=4)
                if q == 0:
                    stats()
                if q == 5:
                    stats()
            with pe.Fori(0, 2) as i:
                for k in range(2):
                    block_fm(AT["xq"] // 2 + i, k, act, (act_ready, 44), offset=4)
            pe.wait_ge(block_used, used(AT["xq"] + 3))
            attention(L2, L3)
            pe.wait_ge(out_lo, outs_before[L3])
            with pe.Fori(0, 2) as i:
                for k in range(2):
                    block_fm(AT["xo"] // 2 + i, k, act, offset=4)
            stats()
            stats()
            ffn(2, AT["ffn3"], 52, offset=4)
            stats()

        @block.scalar
        def _(act):
            norms = [0]
            count = {"normed": 0}

            def fn(out, in_, func=ACT.Copy, **kw):
                return nc.scalar.activation(out, in_, func, **kw)

            def wait(steps, name):
                act.wait_ge(steps.sem, steps.at(name))

            def hi(p, k):
                act.wait_ge(raw_in[k], 16 * (p + 1))
                act.wait_ge(block_done, 2 * p + k + 1)
                fn(w_hi[k][:], raw[k][:]).then_inc(split_hi, 1)

            def hi_next(b):
                if b + 1 < NB:
                    hi((b + 1) // 2, (b + 1) % 2)

            def squares(t, src, n=S):
                nn = norms[0]
                if t == 0:
                    if nn:
                        act.wait_ge(ms_ready, nn)
                    fn(sumsq[:, 0:n], src, ACT.Square).then_inc(sq_ready, 1)
                    return
                if t >= 3 or nn:
                    act.wait_ge(sumsq_step, max(7 * nn, 7 * nn + t - 2))
                fn(square[t % 2][:, 0:n], src, ACT.Square).then_inc(sq_ready, 1)

            def take_root(blocks=NT):
                act.wait_ge(ms_ready, norms[0] + 1)
                fn(root[:, 0:blocks], ps[:, 4, 0:blocks], ACT.Sqrt, bias=eps[:, 0:1],
                   scale=1.0 / D).then_inc(root_ready, 1)
                norms[0] += 1

            def prenorm(shift, gain):
                for t in range(DT):
                    act.wait_ge(normed_ready, count["normed"] + 1)
                    kw = dict(scale=gain[:, t:t + 1])
                    if shift is not None:
                        kw["bias"] = shift[:, t:t + 1]
                    fn(act_hi[:, t, :], normed[t % 2][:], ACT.Identity, **kw)
                    fn(act32[t % 2][:], normed[t % 2][:], ACT.Identity, **kw).then_inc(act32_ready, 1)
                    count["normed"] += 1

            def ffn(b0, source):
                for third, n in enumerate(THIRDS):
                    s = (b0 + 12 * third) // 2
                    with act.Fori(0, n // 2) as i:
                        for k in range(2):
                            hi(s + i + k, 1 - k)
                            act.wait_ge(block_done, 2 * (s + i) + k + START + 1)
                            fn(silu[k][:], ps[:, 2 * k, :], ACT.Silu).then_inc(silu_ready, 1)
                    s += n // 2
                    if third < 2:
                        with act.Fori(0, 2) as i:
                            for k in range(2):
                                hi(s + i + k, 1 - k)
                    else:
                        residual_squares(2 * s, source)

            def residual_squares(b0, source, between=None):
                for q in range(4):
                    b = b0 + q
                    if between is None or q:
                        hi_next(b)
                    if between is not None:
                        between(2 * q)
                        between(2 * q + 1)
                    act.wait_ge(block_used, used(b))
                    for t in (2 * q, 2 * q + 1):
                        squares(t, source[:, t, :])

            def attention(g0, g1, fill=None):
                def exps(g):
                    act.wait_ge(negmax_ready, g + 1)
                    nk = nkeys(g)
                    for a in range(2):
                        last = fn(sc(g)[:, a, 0:nk], sc(g)[:, a, 0:nk], ACT.Exp,
                                  bias=nmx[g % 3][:, a:a + 1], accum_out=den[g % 3][:, a:a + 1])
                    if items[g][0] == "local":
                        last = fn(sinke[g % 3][:], sinkd[g % 3][:], ACT.Exp)
                    last.then_inc(exp_done, 1)

                def copy_a(g):
                    act.wait_ge(turned, g + 1)
                    if g - g0 >= 2:
                        act.wait_ge(pv_done, g - 1)
                    rows, width = min(nkeys(g), P), P * len(key_tiles(g))
                    fn(pt(g)[0:rows, 0, 0:width], ps[0:rows, 4, 0:width]).then_inc(turned_a, 1)

                def outs(g):
                    target = hid_hi if items[g][0] == "local" else act_hi
                    for t, bank in out_tiles(g):
                        act.wait_ge(pv_done, g + 1)
                        fn(target[:, t, :], ps[:, bank, :]).then_inc(out_hi, 1)

                exps(g0)
                for g in range(g0, g1):
                    if g + 1 < g1:
                        exps(g + 1)
                    copy_a(g)
                    if g > g0:
                        outs(g - 1)
                    m, quarter = divmod(g - g0, 8)
                    if fill is not None and quarter < 4:
                        p, k = divmod(fill + m + 1, 2)
                        if quarter == 0:
                            act.wait_ge(raw_in[k], 16 * (p + 1))
                            act.wait_ge(block_done, 2 * p + k + 1)
                        cut = slice(2 * quarter, 2 * quarter + 2)
                        last = fn(w_hi[k][:, cut, :], raw[k][:, cut, :])
                        if quarter == 3:
                            last.then_inc(split_hi, 1)
                outs(g1 - 1)

            act.dma_start(cols[:], ten["cols"]).then_inc(cols_in, 16)
            act.dma_start(consts[:], ten["consts"]).then_inc(consts_in, 16)
            act.dma_start(selector[:], ten["selector"]).then_inc(sel_in, 16)
            act.dma_start(rel[0:32, :], ten["rel"]).then_inc(rel_in, 16)
            for e, name in enumerate(("w2k", "w2v")):
                act.dma_start(w2[:, e], ten[name].rearrange("(i p) n -> p i n", p=P)).then_inc(w2_in, 16)
            act.wait_ge(cols_in, 16)
            fn(c_act[:], col("c", 0, DT), ACT.Silu).then_inc(c_ready, 1)
            act.wait_ge(x_in, 16)
            act.wait_ge(filled, 1)
            for t in range(DT):
                squares(t, x[:, t, :])
            for h in range(8):
                act.wait_ge(brow_sum, h + 1)
                if h >= 2:
                    act.wait_ge(brow_out[h % 2], 16 * (h // 2))
                fn(biasrow[h % 2][:], ps[:, 2:4, :].rearrange("p a n -> p (a n)")[:, 0:NDIST]) \
                    .then_inc(brow_copied, 1)
                act.wait_ge(brow_copied, h + 1)
                act.dma_start(scratch[h], biasrow[h % 2][:]).then_inc(brow_out[h % 2], 16)
            take_root()
            hi(0, 0)
            act.wait_ge(mods_ready, 1)
            for k in range(2):
                act.wait_ge(brow_out[k], 64)
            prenorm(mods[:, 0:8], gains[:, 0])
            ffn(AT["ffn1"], x)

            take_root()
            act.wait_ge(mods_ready, 2)
            prenorm(mods[:, 24:32], gains[:, 1])
            for i in range(4):
                for u in range(2):
                    b = AT["conv"] + 3 * i + u
                    hi_next(b)
                    act.wait_ge(block_done, done(b))
                    fn(cgate[u][:], ps[:, 2 * (b % 2), :]).then_inc(cgate_ready, 1)
                hi_next(b + 1)

            with act.Fori(0, 4) as i:
                for k in range(2):
                    hi(AT["zconv"] // 2 + i + k, 1 - k)
                    act.wait_ge(block_done, 2 * i + AT["zconv"] + k + START + 1)
                    fn(sig[k][:], ps[:, 2 * k, :], ACT.Sigmoid).then_inc(sig_ready, 1)
            for r in range(5):
                b = AT["q"] + r
                hi_next(b)
                act.wait_ge(block_done, done(b))
                if r == 0:
                    act.wait_ge(block_used, used(b - 1))
                if r >= 2:
                    act.wait_ge(rot_sum, r - 1)
                fn(unrot[b % 2][:], ps[:, 2 * (b % 2):2 * (b % 2) + 2, :],
                   scale=HD ** -0.5 if r < 4 else 1.0).then_inc(unrot_ready, 1)
            hi_next(AT["v"])
            attention(0, L1, AT["za"])
            hi_next(AT["attnproj"])
            act.wait_ge(block_used, used(AT["attnproj"] - 1))
            fn(q1[:], q1[:], ACT.Sigmoid).then_inc(sig_ready, 1)
            for q in range(1, 4):
                hi_next(AT["attnproj"] + q)
            for t in range(DT):
                act.wait_ge(merged_ready, t // 2 + 1)
                fn(act_hi[:, t, :], y[:, t, :]).then_inc(merged_hi, 1)
            residual_squares(AT["out1"], x)
            take_root()
            prenorm(mods[:, 48:56], gains[:, 2])
            ffn(AT["ffn2"], x)

            take_root()
            for t in range(DT):
                act.wait_ge(x_ready, t + 1)
                squares(t, x[:, t, :])
            take_root()
            prenorm(None, col("mixpre", 0, DT))
            b = AT["misc"]
            hi_next(b)
            act.wait_ge(block_used, used(b))
            fn(gsig[:], irow[:], ACT.Sigmoid).then_inc(ca.sem, ca.one("gsig"))
            hi_next(AT["kvc"])
            hi_next(AT["vv"])
            wait(cp, "gateT")
            fn(gT[:], ps[:, 6, :].rearrange("p (i n) -> p i n", n=P)).then_inc(ca.sem, ca.one("gT"))
            wait(cp, "swap")
            fn(kvs[:], ps[:, 4:6, :]).then_inc(ca.sem, ca.one("kvs"))
            hi_next(AT["kk"])
            for e in range(2):
                hi_next(AT["nq"] + e)
                wait(cd, f"cb{e}")
                fn(cb_hi[e][:], cb[:]).then_inc(ca.sem, ca.one(f"hi{e}"))
            for e, name in enumerate(("mq", "mk")):
                hi_next(AT[name])
                wait(cd, f"conv{e}")
                for u in range(2):
                    last = fn(mqk[:, 2 * e + u, :], usum[:, u, :], ACT.Silu,
                              bias=col("conv2b", 2 * e + u))
                last.then_inc(ca.sem, ca.one(name))
            hi_next(AT["mv"])
            hi_next(AT["mv"] + 1)
            for e in range(2):
                hi_next(AT["mo"] + e)
                act.wait_ge(block_used, used(AT["mo"] + e))
                fn(mo[:, 2 * e:2 * e + 2, :], mo[:, 2 * e:2 * e + 2, :], ACT.Sigmoid) \
                    .then_inc(ca.sem, ca.one(f"mo{e}"))
            for e in range(2):
                hi_next(AT["cmp"] + 2 * e)
                hi_next(AT["cmp"] + 2 * e + 1)
                act.wait_ge(block_done, done(AT["cmp"] + 2 * e + 1))
                fn(hc[0:62, e, :], ps[0:62, 4 + e, 0:256], ACT.Silu) \
                    .then_inc(ca.sem, ca.one(f"hidden{e}"))
            wait(cp, "hiddenT")
            fn(hcT[:].rearrange("p e i n -> p (e i) n"),
               ps[:, 6, 0:256].rearrange("p (a n) -> p a n", n=64)[:, :, 0:62]) \
                .then_inc(ca.sem, ca.one("hiddenT"))
            wait(cd, "vcmp")
            wait(cp, "vcmp")
            for h in range(8):
                row = scratch[h].rearrange("p n -> (p n)")
                skew = row[P - 1:P - 1 + P * (NDIST - 1)].rearrange("(p n) -> p n", n=NDIST - 1)
                act.dma_start(table[:, h, :], skew[:, 0:S]).then_inc(table_in, 16)
            attention(L1, L2)

            wait(md, "nabs")
            fn(run[1][:], run[0][:], ACT.Exp).then_inc(ma.sem, ma.one("exp"))
            wait(ma, "exp")
            fn(arow[:], run[1][:], ACT.Ln, bias=ones[:, 0:1]).then_inc(ma.sem, ma.one("ln"))
            wait(mp, "lfT")
            fn(lfT[:], ps[:, 0, :].rearrange("p (i n) -> p i n", n=P)).then_inc(ma.sem, ma.one("lfT"))
            wait(mp, "aT")
            fn(aT[:], ps[:, 0, :].rearrange("p (i n) -> p i n", n=P)).then_inc(ma.sem, ma.one("aT"))
            wait(md, "nem")
            fn(emrow[:], emrow[:], ACT.Exp).then_inc(ma.sem, ma.one("em"))
            wait(ma, "aT")
            for h in heads4:
                wait(mp, f"max{h}")
                if h >= 2:
                    wait(md, f"diag{h - 2}3")
                    wait(ma, f"w{h - 2}3")
                fn(nmax[h % 2][:], ps[:, 2, :], scale=-1.0).then_inc(ma.sem, ma.one(f"nmax{h}"))
                wait(ma, f"nmax{h}")
                for kb in range(NT):
                    c, t0 = 4 * h + kb, kb * P
                    wait(md, f"diag{h}{kb}")
                    if c >= 2:
                        wait(mp, f"value{(c - 2) // 4}{(c - 2) % 4}")
                    a = aT[:, kb, 32 * h:32 * h + 1]
                    last = fn(wt[c % 2][:, t0:t0 + P], diag[c % 2][:], ACT.Exp, bias=a)
                    if kb < NT - 1:
                        last = fn(wt[c % 2][:, t0 + P:S], nmax[h % 2][:, t0 + P:S], ACT.Exp, bias=a)
                    last.then_inc(ma.sem, ma.one(f"w{h}{kb}"))
                wait(mp, f"value{h}3")
                fn(num[:, h, :], ps[:, 6, :]).then_inc(ma.sem, ma.one(f"num{h}"))
            fn(drow[:], ps[:, 7, :]).then_inc(ma.sem, ma.one("den"))
            for h in heads4:
                wait(md, f"h{h}")
                fn(square4[h][:], num[:, h, :], ACT.Square).then_inc(ma.sem, ma.one(f"square{h}"))
            wait(mp, "sum3")
            fn(drow[:], ps[:, 3, :], ACT.Sqrt, bias=eps[:, 0:1], scale=1.0 / P) \
                .then_inc(ma.sem, ma.one("root"))
            for h in heads4:
                wait(md, f"m{h}")
                fn(act_hi[:, 4 + h, :], num[:, h, :]).then_inc(ma.sem, ma.one(f"hi{h}"))

            act.wait_ge(act_ready, 44)
            act.dma_start(mt[:], ten["mem"]).then_inc(mem_in, 16)
            act.wait_ge(mem_in, 16)
            for t in range(DT):
                squares(t, mt[:, t, :], MEM)
            hi_next(AT["out2"])
            take_root(MEM // P)

            def memory_high(t):
                act.wait_ge(normed_ready, count["normed"] + 1)
                fn(mn_hi[:, t, :], mem32[t % 2][:]).then_inc(mem_hi, 1)
                count["normed"] += 1

            residual_squares(AT["out2"], y, between=memory_high)
            hi_next(AT["memk"])
            take_root()
            for q in range(1, 8):
                hi_next(AT["memk"] + q)
                if 1 <= q <= 4:
                    for t in (2 * q - 2, 2 * q - 1):
                        act.wait_ge(x_ready, DT + t + 1)
                        squares(t, x[:, t, :])
                if q == 5:
                    take_root()
            prenorm(None, col("xpre", 0, DT))
            for q in range(4):
                hi_next(AT["xq"] + q)
            attention(L2, L3)
            residual_squares(AT["xo"], y)
            take_root()
            for t in range(DT):
                act.wait_ge(x_ready, 2 * DT + t + 1)
                squares(t, x[:, t, :])
            take_root()
            prenorm(None, col("fpre", 0, DT))
            ffn(AT["ffn3"], y)
            take_root()

        @block.vector
        def _(dve):
            norms = [0]
            count = {"step": 0, "act32": 0, "silu": 0}
            v = nc.vector

            def wait(steps, name):
                dve.wait_ge(steps.sem, steps.at(name))

            def link(ins):
                ins.then_inc(v_step, 1)
                count["step"] += 1
                dve.wait_ge(v_step, count["step"])

            def lo(p, k):
                dve.wait_ge(split_hi, 2 * p + k + 1)
                v.tensor_tensor(w_lo[k][:], raw[k][:], w_hi[k][:].bitcast(F32),
                                ALU.subtract).then_inc(split_lo, 1)

            def lo_next(b):
                if b + 1 < NB:
                    lo((b + 1) // 2, (b + 1) % 2)

            def banks(b):
                return ps[:, 2 * (b % 2):2 * (b % 2) + 2, :]

            def add_squares(t, n=S):
                nn = norms[0]
                if t == 0:
                    return
                dve.wait_ge(sq_ready, DT * nn + t + 1)
                if t > 1:
                    dve.wait_ge(sumsq_step, 7 * nn + t - 1)
                v.tensor_tensor(sumsq[:, 0:n], sumsq[:, 0:n], square[t % 2][:, 0:n],
                                ALU.add).then_inc(sumsq_step, 1)

            def invert(blocks=NT):
                dve.wait_ge(root_ready, norms[0] + 1)
                v.reciprocal(rinv[:, 0:blocks], root[:, 0:blocks]).then_inc(rinv_ready, 1)
                dve.wait_ge(rstd_ready, norms[0] + 1)
                norms[0] += 1

            def prenorm():
                def low(t):
                    dve.wait_ge(act32_ready, count["act32"] - DT + t + 1)
                    v.tensor_tensor(act_lo[:, t, :], act32[t % 2][:], act_hi[:, t, :].bitcast(F32),
                                    ALU.subtract).then_inc(act_ready, 1)

                count["act32"] += DT
                for t in range(DT):
                    if t >= 2:
                        low(t - 2)
                    v.tensor_tensor(normed[t % 2][:], x[:, t, :], ps[:, 5, :],
                                    ALU.mult).then_inc(normed_ready, 1)
                low(DT - 2)
                low(DT - 1)

            def post(t, name):
                link(v.scalar_tensor_tensor(out=normed[t % 2][:], in0=y[:, t, :], scalar=col(name, t),
                                            in1=ps[:, 5, :], op0=ALU.mult, op1=ALU.mult))
                v.tensor_tensor(x[:, t, :], x[:, t, :], normed[t % 2][:],
                                ALU.add).then_inc(x_ready, 1)

            def tiles2(ap, m):
                return ap[:, m:m + 2, :] if isinstance(m, int) else ap[:, bass.ds(m, 2), :]

            def update(p, k, m, gate, third):
                dve.wait_ge(block_done, 2 * p + k + START + 1)
                if gate is None:
                    out, sums = tiles2(y, m), ps[:, 2 * k:2 * k + 2, :]
                    if third == 0:
                        v.tensor_copy(out, sums).then_inc(block_used, 1)
                    else:
                        v.tensor_tensor(out, out, sums, ALU.add).then_inc(block_used, 1)
                    return
                for u in range(2):
                    at = slice(m + u, m + u + 1) if isinstance(m, int) else bass.ds(m + u, 1)
                    tile = x[:, at, :].rearrange("p a n -> p (a n)")
                    last = v.scalar_tensor_tensor(out=tile, in0=ps[:, 2 * k + u, :],
                                                  scalar=gate[:, at], in1=tile,
                                                  op0=ALU.mult, op1=ALU.add)
                last.then_inc(block_used, 1)

            def final_updates(b0, gate, third=2, between=None):
                for q in range(4):
                    b = b0 + q
                    if between is None or q:
                        lo_next(b)
                    if between is not None:
                        between(2 * q)
                        between(2 * q + 1)
                    update(b // 2, b % 2, 2 * q, gate, third)
                    add_squares(2 * q)
                    add_squares(2 * q + 1)

            def ada_start(g):
                if g >= 2:
                    dve.wait_ge(ada_sum, g - 1)
                v.memset(ada_acc[g % 2][:], 0.0).then_inc(ada_zero, 1)
                dve.wait_ge(ada_zero, g + 1)

            def ada_block(g, i, k):
                dve.wait_ge(ada_in[k], 16 * (2 * g + i + 1))
                for u in range(2):
                    t = 4 * i + 2 * k + u
                    at = slice(t, t + 1) if isinstance(t, int) else bass.ds(t, 1)
                    dve.wait_ge(ada_step, DT * g + t)
                    v.scalar_tensor_tensor(out=ada_acc[g % 2][:], in0=ada_raw[k][:, u, :],
                                           scalar=c_act[:, at], in1=ada_acc[g % 2][:],
                                           op0=ALU.mult, op1=ALU.add).then_inc(ada_step, 1)

            def modulation(first, end):
                dve.wait_ge(ada_sum, end)
                cut = slice(8 * first, 8 * end)
                link(v.tensor_tensor(mods[:, cut], ps[:, 7, cut], col("b_ada", 8 * first, 8 * (end - first)),
                                     ALU.add))

            def gain(i, scale, name):
                return v.scalar_tensor_tensor(out=gains[:, i, :], in0=mods[:, 8 * scale:8 * scale + 8],
                                              scalar=1.0, in1=col(name, 0, DT), op0=ALU.add,
                                              op1=ALU.mult)

            def ffn(b0, gate, ada=False):
                offset = 4 if gate is None else 0
                groups = iter(range(2, 9) if ada else [])
                for third, n in enumerate(THIRDS):
                    s = (b0 + 12 * third) // 2
                    per = 2
                    steps = count["step"]
                    for first, end in gu_loops(n, ada):
                        g = next(groups, None)
                        if g is not None:
                            ada_start(g)
                        with dve.Fori(first, end) as i:
                            for k in range(2):
                                b = 2 * (s + i) + k
                                lo(s + i + k, 1 - k)
                                if g is not None:
                                    ada_block(g, i - first, k)
                                dve.wait_ge(silu_ready, count["silu"] + 2 * i + k + 1)
                                v.tensor_tensor(prod[k][:], silu[k][:], ps[:, 2 * k + 1, :],
                                                ALU.mult).then_inc(block_used, 1)
                                dve.wait_ge(block_used, b + START + 1 - offset)
                                at = bass.ds(2 * i + k, 1)
                                hi_tile = hid_hi[:, at, :].rearrange("p a n -> p (a n)")
                                lo_tile = hid_lo[:, at, :].rearrange("p a n -> p (a n)")
                                v.tensor_scalar(hi_tile, prod[k][:], 1.0, None,
                                                ALU.mult).then_inc(v_step, 1)
                                dve.wait_ge(v_step, steps + per * i + k + 1)
                                v.tensor_tensor(lo_tile, prod[k][:], hi_tile.bitcast(F32),
                                                ALU.subtract).then_inc(hid_ready, 1)
                    count["step"] += per * (n // 2)
                    count["silu"] += n
                    s += n // 2
                    if ada and third == 0:
                        modulation(2, 3)
                        link(v.tensor_scalar(gains[:, 3, :], mods[:, 16:24], 0.5, None, ALU.mult))
                    if third < 2:
                        g = next(groups, None)
                        if g is not None:
                            ada_start(g)
                        with dve.Fori(0, 2) as i:
                            for k in range(2):
                                lo(s + i + k, 1 - k)
                                if g is not None:
                                    ada_block(g, i, k)
                                update(s + i, k, 4 * i + 2 * k, gate, third)
                    else:
                        final_updates(2 * s, gate)

            def attention(g0, g1, fill=None, halves=0, take_half=None):
                def bias(g):
                    ph, j, n, br = items[g]
                    nk = nkeys(g)
                    dve.wait_ge(scores_ready, g + 1)
                    if g - g0 >= 3:
                        dve.wait_ge(turned, g - 2)
                    for a in range(2):
                        if ph == "local":
                            add = const("mask")[:, 256 - nk:256]
                        elif ph == "sparse":
                            first = P * (NT - 1 - n)
                            row = table[:, j + 4 * a, :]
                            add = row[:, first + 31:S:16] if br == 0 else row[:, first:S]
                        else:
                            add = zeros[:, 0:nk]
                        last = v.tensor_tensor_reduce(sc(g)[:, a, 0:nk],
                                                      ps[:, scores_of(g) + a, 0:nk], add, 1.0, -3e38,
                                                      ALU.add, ALU.max, smax[g % 3][:, a:a + 1])
                    last.then_inc(biased, 1)
                    dve.wait_ge(biased, g + 1)
                    if ph == "local":
                        sink = negsink[:, 2 * j:2 * j + 2]
                        link(v.scalar_tensor_tensor(out=nmx[g % 3][:], in0=smax[g % 3][:], scalar=-1.0,
                                                    in1=sink, op0=ALU.mult, op1=ALU.min))
                        v.tensor_tensor(sinkd[g % 3][:], nmx[g % 3][:], sink,
                                        ALU.subtract).then_inc(negmax_ready, 1)
                    else:
                        v.tensor_scalar(nmx[g % 3][:], smax[g % 3][:], -1.0, None,
                                        ALU.mult).then_inc(negmax_ready, 1)

                def norm(g):
                    ph, j, n, br = items[g]
                    dve.wait_ge(exp_done, g + 1)
                    total, w = den[g % 3], inv[g % 3]
                    if ph == "local":
                        link(v.tensor_tensor(total[:], total[:], sinke[g % 3][:], ALU.add))
                    link(v.reciprocal(w[:], total[:]))
                    if ph == "sparse":
                        gate = gT[:, n, 1 + 3 * j + br:14 + 3 * j + br:12]
                        if n == 0 and br == 0:
                            link(v.scalar_tensor_tensor(out=w[:], in0=w[:], scalar=const("valid"),
                                                        in1=gate, op0=ALU.mult, op1=ALU.mult))
                        else:
                            link(v.tensor_tensor(w[:], w[:], gate, ALU.mult))
                    nk = nkeys(g)
                    for a in range(2):
                        last = v.tensor_scalar(sc(g)[:, a, 0:nk], sc(g)[:, a, 0:nk], w[:, a:a + 1],
                                               None, ALU.mult)
                    last.then_inc(probs_ready, 1)

                def copy_b(g):
                    dve.wait_ge(turned, g + 1)
                    if g - g0 >= 2:
                        dve.wait_ge(pv_done, g - 1)
                    rows, width = min(nkeys(g), P), P * len(key_tiles(g))
                    v.tensor_copy(pt(g)[0:rows, 1, 0:width],
                                  ps[0:rows, 5, 0:width]).then_inc(turned_b, 1)

                def outs(g):
                    hi_to, lo_to = (hid_hi, hid_lo) if items[g][0] == "local" else (act_hi, act_lo)
                    for i, (t, bank) in enumerate(out_tiles(g)):
                        dve.wait_ge(out_hi, outs_before[g] + i + 1)
                        v.tensor_tensor(lo_to[:, t, :], ps[:, bank, :], hi_to[:, t, :].bitcast(F32),
                                        ALU.subtract).then_inc(out_lo, 1)

                bias(g0)
                bias(g0 + 1)
                norm(g0)
                for g in range(g0, g1):
                    if g > g0:
                        copy_b(g - 1)
                    if g + 2 < g1:
                        bias(g + 2)
                    if g + 1 < g1:
                        norm(g + 1)
                    if g > g0 + 1:
                        outs(g - 2)
                    if fill is not None:
                        m, u, c = fill_half(g - g0)
                        if (g - g0) % 8 in (4, 5):
                            p, k = divmod(fill + m + 1, 2)
                            if c == 0:
                                dve.wait_ge(split_hi, 2 * p + k + 1)
                            cut = slice(4 * c, 4 * c + 4)
                            last = v.tensor_tensor(w_lo[k][:, cut, :], raw[k][:, cut, :],
                                                   w_hi[k][:, cut, :].bitcast(F32), ALU.subtract)
                            if c == 1:
                                last.then_inc(split_lo, 1)
                        if c == 3:
                            if u == 0:
                                dve.wait_ge(half_done, halves + m + 1)
                                take_half(2 * m).then_inc(half_used, 1)
                            else:
                                dve.wait_ge(block_done, done(fill + m))
                                take_half(2 * m + 1).then_inc(block_used, 1)
                copy_b(g1 - 1)
                outs(g1 - 2)
                outs(g1 - 1)

            v.memset(ones[:], 1.0)
            v.memset(zeros[:], 0.0)
            v.memset(eps[:], EPS).then_inc(filled, 1)
            dve.wait_ge(filled, 1)
            dve.wait_ge(rel_in, 16)
            link(v.memset(rel[32:33, :], 1.0))
            for h in range(8):
                last = v.tensor_scalar(relb[:, h, :], ones[0:33, :], rel[:, h:h + 1], None, ALU.mult)
            last.then_inc(relb_ready, 1)
            for t in range(DT):
                add_squares(t)
            for k in range(START):
                v.memset(nmx[k][:], 0.0).then_inc(block_used, 1)
            dve.wait_ge(c_ready, 1)
            for g in range(2):
                ada_start(g)
                for i in range(2):
                    for k in range(2):
                        ada_block(g, i, k)
            modulation(0, 2)
            v.tensor_scalar(negsink[:], col("sinks", 0, 16), -1.0, None, ALU.mult)
            gain(0, 1, "g_ffn1").then_inc(mods_ready, 1)
            invert()
            prenorm()
            lo(0, 0)
            ffn(AT["ffn1"], gains[:, 3], ada=True)
            modulation(3, 9)
            gain(1, 4, "g_mix")
            gain(2, 7, "g_ffn2")
            v.tensor_scalar(gains[:, 4, :], mods[:, 64:72], 0.5, None, ALU.mult) \
                .then_inc(mods_ready, 1)

            invert()
            prenorm()
            for u in range(2):
                last = v.memset(cu[u][:, 0:2], 0.0)
            link(last)
            for i in range(4):
                for u in range(2):
                    b = AT["conv"] + 3 * i + u
                    lo_next(b)
                    dve.wait_ge(cgate_ready, 2 * i + u + 1)
                    v.tensor_tensor(cu[u][:, 2:], cgate[u][:], ps[:, 2 * (b % 2) + 1, :],
                                    ALU.mult).then_inc(block_used, 1)
                    dve.wait_ge(block_used, used(b))
                    j = 2 * i + u
                    link(v.tensor_scalar(conv[u][:], cu[u][:, 0:S], col("conv", j), None, ALU.mult))
                    for tap in (1, 2):
                        link(v.scalar_tensor_tensor(out=conv[u][:], in0=cu[u][:, tap:tap + S],
                                                    scalar=col("conv", 8 * tap + j), in1=conv[u][:],
                                                    op0=ALU.mult, op1=ALU.add))
                b = AT["conv"] + 3 * i + 2
                lo_next(b)
                dve.wait_ge(block_done, done(b))
                for u in range(2):
                    last = v.tensor_tensor(bconv[u][:], conv[u][:], ps[:, 2 * (b % 2) + u, :], ALU.mult)
                last.then_inc(block_used, 1)
                dve.wait_ge(block_used, used(b))
                for u in range(2):
                    link(v.tensor_scalar(hid_hi[:, 2 * i + u, :], bconv[u][:], 1.0, None, ALU.mult))
                    v.tensor_tensor(hid_lo[:, 2 * i + u, :], bconv[u][:],
                                    hid_hi[:, 2 * i + u, :].bitcast(F32),
                                    ALU.subtract).then_inc(hid_ready, 1)
            with dve.Fori(0, 4) as i:
                for k in range(2):
                    lo(AT["zconv"] // 2 + i + k, 1 - k)
                    dve.wait_ge(sig_ready, 2 * i + k + 1)
                    tile = y[:, bass.ds(2 * i + k, 1), :].rearrange("p a n -> p (a n)")
                    v.tensor_tensor(tile, sig[k][:], ps[:, 2 * k + 1, :],
                                    ALU.mult).then_inc(block_used, 1)

            def rope(r, b):
                out = q1[:, 2 * r:2 * r + 2, :] if r < 4 else k1[:]
                dve.wait_ge(rot_sum, r + 1)
                sin = const("sin").unsqueeze(1).to_broadcast([P, 2, S])
                link(v.tensor_tensor(out, ps[:, 4:6, :], sin, ALU.mult))
                v.tensor_tensor(out, out, rcos[:], ALU.add).then_inc(rope_done, 1)

            for r in range(5):
                b = AT["q"] + r
                lo_next(b)
                if r:
                    rope(r - 1, b - 1)
                dve.wait_ge(unrot_ready, r + 1)
                if r:
                    dve.wait_ge(rope_done, r)
                cos = const("cos").unsqueeze(1).to_broadcast([P, 2, S])
                v.tensor_tensor(rcos[:], unrot[b % 2][:], cos, ALU.mult).then_inc(block_used, 1)
                dve.wait_ge(block_used, used(b))
            b = AT["v"]
            lo_next(b)
            dve.wait_ge(block_done, done(b))
            v.tensor_copy(v1[:].rearrange("p i n -> p (i n)"),
                          banks(b).rearrange("p a n -> p (a n)")).then_inc(block_used, 1)
            rope(4, b - 1)
            attention(0, L1, AT["za"], take_half=lambda i: v.tensor_copy(q1[:, i, :], ps[:, 7, :]))
            for q in range(4):
                b = AT["attnproj"] + q
                lo_next(b)
                dve.wait_ge(block_done, done(b))
                if q == 0:
                    dve.wait_ge(sig_ready, 9)
                gate = q1[:, 2 * q:2 * q + 2, :]
                v.tensor_tensor(gate, gate, banks(b), ALU.mult).then_inc(block_used, 1)
                dve.wait_ge(block_used, used(b))
                tile = y[:, 2 * q:2 * q + 2, :]
                v.tensor_tensor(tile, tile, gate, ALU.add).then_inc(merged_ready, 1)
            for t in range(DT):
                dve.wait_ge(merged_hi, t + 1)
                v.tensor_tensor(act_lo[:, t, :], y[:, t, :], act_hi[:, t, :].bitcast(F32),
                                ALU.subtract).then_inc(act_ready, 1)
            final_updates(AT["out1"], mods[:, 40:48])
            invert()
            prenorm()
            ffn(AT["ffn2"], gains[:, 4])

            invert()
            for t in range(DT):
                v.scalar_tensor_tensor(out=x[:, t, :], in0=x[:, t, :], scalar=col("g_final", t),
                                       in1=ps[:, 5, :], op0=ALU.mult,
                                       op1=ALU.mult).then_inc(x_ready, 1)
            for t in range(DT):
                add_squares(t)
            invert()
            prenorm()
            link(v.memset(upad[:, :, 0:3], 0.0))
            b = AT["misc"]
            lo_next(b)
            dve.wait_ge(block_done, done(b))
            v.tensor_scalar(irow[:], ps[:, 0, :], col("gate_bias", 0), None, ALU.add)
            v.tensor_scalar(frow[:], ps[:, 1, :], col("gate_bias", 1), None,
                            ALU.add).then_inc(block_used, 1)

            def take(b, out, scale=None):
                lo_next(b)
                dve.wait_ge(block_done, done(b))
                if scale is None:
                    ins = v.tensor_copy(out, banks(b))
                else:
                    ins = v.tensor_scalar(out, banks(b), scale, None, ALU.mult)
                ins.then_inc(block_used, 1)

            def quarters(b):
                return banks(b).rearrange("p a (c n) -> p (a c) n", n=256)

            take(AT["kvc"], kvc[:])
            b = AT["vv"]
            lo_next(b)
            dve.wait_ge(block_done, done(b))
            v.tensor_copy(vv[:], quarters(b)).then_inc(block_used, 1)
            take(AT["kk"], kk[:])
            for e in range(2):
                take(AT["nq"] + e, nq[:, 2 * e:2 * e + 2, :], HD ** -0.5)
                if e == 0:
                    wait(ca, "kvs")
                else:
                    wait(cd, "lo0")
                for parity in range(2):
                    half = slice(64 * parity, 64 * parity + 64)
                    for a in range(2):
                        src = (kvc if a == parity else kvs)[half, e, :] \
                            .rearrange("p (c j s) -> p j c s", j=8, s=2)
                        for up in range(2):
                            pos = col("pos_k" if e == 0 else "pos_v", 8 * up, 8)[half, :]
                            last = v.tensor_tensor(
                                cb[half, 8 * up:8 * up + 8, 31 * a:31 * a + 31],
                                src[:, :, up:up + 31, parity],
                                pos.unsqueeze(2).to_broadcast([64, 8, 31]), ALU.add)
                last.then_inc(cd.sem, cd.one(f"cb{e}"))
                wait(ca, f"hi{e}")
                v.tensor_tensor(cb_lo[e][:], cb[:], cb_hi[e][:].bitcast(F32),
                                ALU.subtract).then_inc(cd.sem, cd.one(f"lo{e}"))
            for e, name in enumerate(("mq", "mk")):
                take(AT[name], upad[:, :, 3:])
                dve.wait_ge(block_used, used(AT[name]))
                if e:
                    wait(ca, "mq")
                for u in range(2):
                    j = 2 * e + u
                    link(v.tensor_scalar(usum[:, u, :], upad[:, u, 0:S], col("conv2", j), None,
                                         ALU.mult))
                    for tap in (1, 2, 3):
                        ins = v.scalar_tensor_tensor(out=usum[:, u, :], in0=upad[:, u, tap:tap + S],
                                                     scalar=col("conv2", 4 * tap + j),
                                                     in1=usum[:, u, :], op0=ALU.mult, op1=ALU.add)
                        if u == 1 and tap == 3:
                            ins.then_inc(cd.sem, cd.one(f"conv{e}"))
                        else:
                            link(ins)
            for e in range(2):
                b = AT["mv"] + e
                lo_next(b)
                dve.wait_ge(block_done, done(b))
                v.tensor_copy(mv[:, :, 256 * e:256 * e + 256], quarters(b)).then_inc(block_used, 1)
            wait(ca, "mk")
            v.tensor_scalar(mqk[:, 2:4, :], mqk[:, 2:4, :], HD ** -0.5, None,
                            ALU.mult).then_inc(cd.sem, cd.one("mk"))
            for e in range(2):
                take(AT["mo"] + e, mo[:, 2 * e:2 * e + 2, :])
            for b in range(AT["cmp"], AT["cmp"] + 4):
                lo_next(b)
            wait(cp, "kcmp")
            v.tensor_copy(kcmp[:, 0:31], ps[:, 7, 0:31]).then_inc(cd.sem, cd.one("kcmp"))
            wait(cp, "vcmp")
            v.tensor_copy(vcmp[0:31, :], ps[0:31, 4, 0:P]).then_inc(cd.sem, cd.one("vcmp"))
            dve.wait_ge(table_in, 16 * 8)
            attention(L1, L2)

            v.scalar_tensor_tensor(out=run[0][:], in0=frow[:], scalar=-1.0, in1=frow[:],
                                   op0=ALU.mult, op1=ALU.min).then_inc(md.sem, md.one("nabs"))
            wait(ma, "ln")
            v.scalar_tensor_tensor(out=frow[:], in0=frow[:], scalar=0.0, in1=arow[:],
                                   op0=ALU.min, op1=ALU.subtract).then_inc(md.sem, md.one("lf"))
            wait(mp, "F")
            v.tensor_tensor(arow[:], irow[:], ps[:, 1, :], ALU.subtract) \
                .then_inc(md.sem, md.one("a"))
            wait(md, "a")
            v.tensor_scalar(run[0][:], arow[:], 0.0, None, ALU.max).then_inc(md.sem, md.one("pos"))
            wait(md, "pos")
            for i in range(9):
                src, dst, w = run[i % 2], run[1 - i % 2], 1 << i
                v.tensor_copy(dst[:, 0:w], src[:, 0:w]).then_inc(md.sem, md.one(f"run{i}a"))
                v.tensor_tensor(dst[:, w:], src[:, w:], src[:, 0:S - w], ALU.max) \
                    .then_inc(md.sem, md.one(f"run{i}b"))
                wait(md, f"run{i}b")
            v.scalar_tensor_tensor(out=emrow[:], in0=run[1][:], scalar=-1.0, in1=ps[:, 1, :],
                                   op0=ALU.mult, op1=ALU.subtract).then_inc(md.sem, md.one("nem"))
            for h in heads4:
                wait(ma, f"nmax{h}")
                for kb in range(NT):
                    c, t0 = 4 * h + kb, kb * P
                    if c >= 2:
                        wait(ma, f"w{(c - 2) // 4}{(c - 2) % 4}")
                    v.tensor_tensor(diag[c % 2][:], nmax[h % 2][:, t0:t0 + P], const("maskT"),
                                    ALU.add).then_inc(md.sem, md.one(f"diag{h}{kb}"))
                    wait(mp, f"scores{h}{kb}")
                    wait(ma, f"w{h}{kb}")
                    v.tensor_tensor(wt[c % 2][:, t0:S], ps[:, 4 + c % 2, 0:S - t0], wt[c % 2][:, t0:S],
                                    ALU.mult).then_inc(md.sem, md.one(f"s{h}{kb}"))
            wait(ma, "den")
            v.scalar_tensor_tensor(out=dinv[:], in0=drow[:], scalar=-1.0, in1=drow[:],
                                   op0=ALU.mult, op1=ALU.max).then_inc(md.sem, md.one("nden"))
            wait(md, "nden")
            wait(ma, "em")
            v.tensor_tensor(dinv[:], dinv[:], emrow[:], ALU.max).then_inc(md.sem, md.one("floor"))
            wait(md, "floor")
            v.reciprocal(dinv[:], dinv[:]).then_inc(md.sem, md.one("dinv"))
            for h in heads4:
                wait(mp, f"dinv{h}")
                v.tensor_tensor(num[:, h, :], num[:, h, :], ps[:, h % 2, :], ALU.mult) \
                    .then_inc(md.sem, md.one(f"h{h}"))
            wait(ma, "root")
            v.reciprocal(dinv[:], drow[:]).then_inc(md.sem, md.one("rinv"))

            def mlstm_low(h):
                wait(ma, f"hi{h}")
                v.tensor_tensor(act_lo[:, 4 + h, :], num[:, h, :], act_hi[:, 4 + h, :].bitcast(F32),
                                ALU.subtract).then_inc(act_ready, 1)

            wait(ca, "mo1")
            for h in heads4:
                wait(mp, f"rms{h}")
                v.tensor_tensor(num[:, h, :], num[:, h, :], ps[:, h % 2, :], ALU.mult) \
                    .then_inc(md.sem, md.one(f"n{h}"))
                wait(md, f"n{h}")
                v.scalar_tensor_tensor(out=num[:, h, :], in0=num[:, h, :], scalar=col("mlnorm", h),
                                       in1=mo[:, h, :], op0=ALU.mult, op1=ALU.mult) \
                    .then_inc(md.sem, md.one(f"m{h}"))
                if h:
                    mlstm_low(h - 1)
            mlstm_low(3)

            for t in range(DT):
                add_squares(t, MEM)
            lo_next(AT["out2"])
            invert(MEM // P)

            def memory_tile(t):
                if t >= 2:
                    dve.wait_ge(mem_ready, t - 1)
                v.scalar_tensor_tensor(out=mem32[t % 2][:], in0=mt[:, t, :],
                                       scalar=col("memn", t), in1=ps[:, 5, 0:MEM], op0=ALU.mult,
                                       op1=ALU.mult).then_inc(normed_ready, 1)
                dve.wait_ge(mem_hi, t + 1)
                v.tensor_tensor(mn_lo[:, t, :], mem32[t % 2][:], mn_hi[:, t, :].bitcast(F32),
                                ALU.subtract).then_inc(mem_ready, 1)

            final_updates(AT["out2"], None, 0, between=memory_tile)

            def memory_block(q):
                b = AT["memk"] + q
                lo_next(b)
                dve.wait_ge(block_done, done(b))
                if q < 4:
                    v.tensor_copy(kx[:, 2 * q:2 * q + 2, :], banks(b)[:, :, 0:MEM]) \
                        .then_inc(block_used, 1)
                else:
                    v.tensor_copy(vx[:, :, 256 * (q - 4):256 * (q - 4) + 256],
                                  ps[:, 2 * (b % 2), :].rearrange("p (i n) -> p i n", n=256)) \
                        .then_inc(block_used, 1)

            memory_block(0)
            invert()
            for q in range(1, 8):
                memory_block(q)
                if q <= 4:
                    for t in (2 * q - 2, 2 * q - 1):
                        post(t, "mixpost")
                    for t in (2 * q - 2, 2 * q - 1):
                        add_squares(t)
                if q == 5:
                    invert()
            prenorm()
            for q in range(4):
                take(AT["xq"] + q, qx[:, 2 * q:2 * q + 2, :], MEM ** -0.5)
            attention(L2, L3)
            final_updates(AT["xo"], None, 0)
            invert()
            for t in range(DT):
                post(t, "xpost")
                if t:
                    add_squares(t - 1)
            add_squares(DT - 1)
            invert()
            prenorm()
            ffn(AT["ffn3"], None)
            invert()
            for t in range(DT):
                post(t, "fpost")


def local_head(i):
    j, a = divmod(i, 2)
    return (j // 4) * 8 + 4 * a + j % 4


def sparse_head(i):
    j, a = divmod(i, 2)
    return 4 * a + j


def heads_to_rows(head_of, n):
    return np.concatenate([np.arange(HD) + HD * head_of(i) for i in range(n)])


def tiles(w):
    rows, n = w.shape
    out = np.zeros((P, DT, n), w.dtype)
    out[:, :rows // P] = w.reshape(rows // P, P, n).transpose(1, 0, 2)
    return out


def weight_blocks(a):
    blocks = []

    def add(*parts):
        blocks.append(np.concatenate([tiles(w) for w in parts], axis=2))

    def pairs(w):
        for j in range(0, w.shape[1], 2 * P):
            add(w[:, j:j + 2 * P])

    def ffn(gu, down):
        first = 0
        for n in THIRDS:
            for j in range(first, first + n):
                add(gu[:, j * P:j * P + P], gu[:, FF + j * P:FF + j * P + P])
            pairs(down[first * P:(first + n) * P])
            first += n

    def cut(w, sizes):
        return np.split(w, np.cumsum(sizes)[:-1], axis=1)

    ffn(a["w1_gu"][0], a["w1_down"][0])
    b_g, c_g, u, q, k, v, zc, za = cut(a["w_in"][0], [D, D, D, D, 256, 256, D, D])
    for i in range(4):
        for j in (2 * i, 2 * i + 1):
            add(c_g[:, j * P:j * P + P], u[:, j * P:j * P + P])
        add(b_g[:, 2 * i * P:2 * i * P + 2 * P])
    rows = heads_to_rows(local_head, 16)
    for j in range(DT):
        add(zc[:, j * P:j * P + P], a["w_conv_proj"][0][:, j * P:j * P + P])
    pairs(q[:, rows])
    pairs(k)
    pairs(v)
    pairs(za)
    pairs(a["w_attn_proj"][0][rows])
    pairs(a["w_out"][0])
    ffn(a["w2_gu"][0], a["w2_down"][0])

    nq, kc, vc, ks, vs, kw, vw, gt, mq, mk, mv, mi, mf, mo = cut(
        a["w_in_2"][0], [512] + [128] * 6 + [24, 256, 256, 512, 4, 4, 512])
    misc = np.zeros((D, 2 * P), nq.dtype)
    misc[:, 0:P:32] = mi
    misc[:, 1:25] = gt
    misc[:, P::32] = mf
    add(misc)
    add(kc, vc)
    add(vs, vw)
    add(ks, kw)
    rows = heads_to_rows(sparse_head, 8)
    pairs(nq[:, rows])
    for w in (mq, mk, mv, mo):
        pairs(w)
    for w in (a["cmp_w1_k_2"][0], a["cmp_w1_v_2"][0]):
        add(w[:D])
        add(w[D:])
    w_out = a["w_out_2"][0]
    pairs(np.concatenate([w_out[rows], w_out[512:]]))
    pairs(a["w_xkv_2"][0])
    pairs(a["w_xq_2"][0])
    pairs(a["w_xo_2"][0])
    ffn(a["w_gate_up_2"][0], a["w_down_2"][0])
    assert len(blocks) == NB
    return np.stack(blocks).reshape(-1)


def ada_blocks(w):
    return np.ascontiguousarray(w.reshape(DT // 2, 2, P, 9, D).transpose(3, 0, 2, 1, 4)).reshape(-1)


def columns(a):
    out = np.zeros((P, NCOL), np.float32)

    def put(name, vec):
        part = np.asarray(vec).reshape(-1, P).T
        out[:, CAT[name]:CAT[name] + part.shape[1]] = part

    for name, key in (("c", "c"), ("b_ada", "b_ada"), ("g_ffn1", "g_ffn1"), ("g_mix", "g_mix"),
                      ("g_ffn2", "g_ffn2"), ("g_final", "g_final"), ("conv", "conv_w"),
                      ("mixpre", "mix_norm_pre_2"), ("mixpost", "mix_norm_post_2"),
                      ("xpre", "xattn_norm_pre_2"), ("memn", "mem_norm_2"),
                      ("xpost", "xattn_norm_post_2"), ("fpre", "ffn_norm_pre_2"),
                      ("fpost", "ffn_norm_post_2"), ("conv2", "conv_w_2"), ("conv2b", "conv_b_2"),
                      ("mlnorm", "mlstm_norm_2"), ("pos_k", "cmp_pos_k_2"), ("pos_v", "cmp_pos_v_2")):
        put(name, a[key])
    sinks = a["sinks"][0]
    for i in range(16):
        out[:, CAT["sinks"] + i] = sinks[local_head(i)]
    for i in range(2):
        out[::32, CAT["gate_bias"] + i] = a["mlstm_gate_bias_2"][0, i]
    return out


def constants():
    out = np.zeros((P, NCONST), np.float32)

    def put(name, value):
        out[:, KAT[name]:KAT[name] + value.shape[1]] = value

    p = np.arange(P)
    put("ident", np.eye(P))
    rot = np.zeros((P, P))
    for m in range(P):
        d = m % HD
        src = m + HD // 2 if d < HD // 2 else m - HD // 2
        rot[src, m] = -1.0 if d < HD // 2 else 1.0
    put("rot", rot)
    put("swap", np.eye(P)[(p + 64) % P])
    put("tri", (np.arange(S)[None, :] >= p[:, None]).astype(np.float32))
    freq = (1.0 / np.float32(10000.0) ** (np.arange(0, HD, 2, dtype=np.float32) / np.float32(HD)))
    ang = freq.astype(np.float32)[p % (HD // 2)][:, None] * np.arange(S, dtype=np.float32)[None, :]
    put("cos", np.cos(ang))
    put("sin", np.sin(ang))
    diff = P + p[:, None] - np.arange(2 * P)[None, :]
    put("mask", np.where((diff >= 0) & (diff < P), 0.0, NEG))
    put("maskT", np.where(p[None, :] >= p[:, None], 0.0, NEG))
    put("valid", (p[:, None] >= 31).astype(np.float32))
    return out


def bias_selector():
    buckets, far = 32, 128
    dist = S - 1 - np.arange(NDIST)
    n = np.maximum(dist, 0)
    half = buckets // 2
    nf = np.maximum(n, 1).astype(np.float32)
    large = half + (np.log(nf / half) / np.float32(np.log(far / half)) * half).astype(np.int32)
    bucket = np.where(n < half, n, np.minimum(large, buckets - 1))
    out = np.zeros((33, NDIST), np.float32)
    out[bucket, np.arange(NDIST)] = (dist >= 0)
    out[32] = np.where(dist >= 0, 0.0, NEG)
    return out


def kernel(**inputs):
    from concourse import bacc
    from concourse.bass_utils import run_bass_kernel_spmd

    a = {name: np.asarray(value) for name, value in inputs.items()}
    arrays = {
        "x": np.ascontiguousarray(a["x"][0].T.reshape(DT, P, S).transpose(1, 0, 2)),
        "mem": np.ascontiguousarray(a["mem_2"][0].T.reshape(DT, P, MEM).transpose(1, 0, 2)),
        "ada": ada_blocks(a["w_ada"][0]),
        "weights": weight_blocks(a),
        "cols": columns(a),
        "consts": constants(),
        "selector": bias_selector(),
        "rel": np.ascontiguousarray(a["rel_bias_2"].T),
        "w2k": np.ascontiguousarray(a["cmp_w2_k_2"][0]),
        "w2v": np.ascontiguousarray(a["cmp_w2_v_2"][0]),
    }
    nc = bacc.Bacc("TRN2", target_bir_lowering=False, num_devices=1)
    ten = {name: nc.dram_tensor(f"in_{name}", value.shape, F32, kind="ExternalInput").ap()
           for name, value in arrays.items()}
    ten["out"] = nc.dram_tensor("result", (P, DT, S), F32, kind="ExternalOutput").ap()
    build(nc, ten)
    result = run_bass_kernel_spmd(nc, [{f"in_{name}": value for name, value in arrays.items()}],
                                  core_ids=[0]).results[0]["result"]
    return np.ascontiguousarray(result.transpose(1, 0, 2).reshape(D, S).T)[None]
```
